# Optimizing a Trainium2 kernel written in Bass

```python
import math
import jax, jax.numpy as jnp
from jax import lax
import numpy as np

D_MODEL = 1024
BATCH = 1
SEQ = 256
DEPTH = 1

ATTN_HEADS = 8
HEAD_DIM = 64
ATTN_W = ATTN_HEADS * HEAD_DIM
MOBA_BLOCK = 256
MOBA_TOPK = 3
Q_CHUNK = 64
POOL_GROUPS = 4
POOL_GROUP_W = 128
POOL_W = POOL_GROUPS * POOL_GROUP_W
POOL_WINDOWS = (2, 4, 8, 16)
NUM_BUCKETS = 32
MAX_DISTANCE = 128
D_FF = 2816
CONV_W = 3
EPS = 1e-6
IN_W = 3 * ATTN_W + POOL_W + 2 * D_MODEL


def rms_norm(x, gain):
    xf = x.astype(jnp.float32)
    y = xf * lax.rsqrt(jnp.mean(xf * xf, axis=-1, keepdims=True) + EPS)
    return (y * gain.astype(jnp.float32)).astype(x.dtype)

def t5_bucket(dist):
    max_exact = NUM_BUCKETS // 2
    n = jnp.maximum(dist, 0)
    nf = jnp.maximum(n, 1).astype(jnp.float32)
    large = max_exact + (jnp.log(nf / max_exact) / math.log(MAX_DISTANCE / max_exact)
                         * (NUM_BUCKETS - max_exact)).astype(jnp.int32)
    large = jnp.minimum(large, NUM_BUCKETS - 1)
    return jnp.where(n < max_exact, n, large)

def moba_attention(q, k, v, rel_bias):
    B, H, S, Dh = q.shape
    n_blocks = -(-S // MOBA_BLOCK)
    s_pad = n_blocks * MOBA_BLOCK
    pad = ((0, 0), (0, 0), (0, s_pad - S), (0, 0))
    q = jnp.pad(q, pad)
    k = jnp.pad(k, pad)
    v = jnp.pad(v, pad)
    k_blocks = k.reshape(B, H, n_blocks, MOBA_BLOCK, Dh)
    v_blocks = v.reshape(B, H, n_blocks, MOBA_BLOCK, Dh)
    k_mean = jnp.mean(k_blocks.astype(jnp.float32), axis=3).astype(k.dtype)

    pos = jnp.arange(s_pad)
    q_blk = pos // MOBA_BLOCK
    gate = jnp.einsum('bhsd,bhnd->bhsn', q, k_mean).astype(jnp.float32)
    past = jnp.arange(n_blocks)[None, :] < q_blk[:, None]
    gate = jnp.where(past[None, None], gate, -jnp.inf)
    k_sel = min(MOBA_TOPK, n_blocks)
    _, sel = lax.top_k(gate, k_sel)
    sel_valid = jnp.arange(k_sel)[None, :] < q_blk[:, None]

    n_chunks = s_pad // Q_CHUNK
    q_c = q.reshape(B, H, n_chunks, Q_CHUNK, Dh).transpose(2, 0, 1, 3, 4)
    sel_c = sel.reshape(B, H, n_chunks, Q_CHUNK, k_sel).transpose(2, 0, 1, 3, 4)
    valid_c = sel_valid.reshape(n_chunks, Q_CHUNK, k_sel)
    bias_t = rel_bias.T.astype(jnp.float32)
    b_idx = jnp.arange(B)[:, None, None, None]
    h_idx = jnp.arange(H)[None, :, None, None]
    offs = jnp.arange(MOBA_BLOCK)
    scale = HEAD_DIM ** -0.5
    n_sel = k_sel * MOBA_BLOCK

    def chunk_fn(args):
        ci, qc, selc, validc = args
        qpos = ci * Q_CHUNK + jnp.arange(Q_CHUNK)
        own = (ci * Q_CHUNK) // MOBA_BLOCK
        k_own = lax.dynamic_index_in_dim(k_blocks, own, axis=2, keepdims=False)
        v_own = lax.dynamic_index_in_dim(v_blocks, own, axis=2, keepdims=False)
        dist_own = qpos[:, None] - (own * MOBA_BLOCK + offs)[None, :]
        bias_own = bias_t[:, t5_bucket(dist_own)]
        logit_own = jnp.einsum('bhqd,bhkd->bhqk', qc, k_own).astype(jnp.float32) * scale + bias_own
        logit_own = jnp.where(dist_own >= 0, logit_own, -jnp.inf)
        k_g = k_blocks[b_idx, h_idx, selc]
        v_g = v_blocks[b_idx, h_idx, selc]
        kpos_sel = selc[..., None] * MOBA_BLOCK + offs
        dist_sel = qpos[None, None, :, None, None] - kpos_sel
        bias_sel = bias_t[h_idx[..., None], t5_bucket(dist_sel)]
        logit_sel = jnp.einsum('bhqd,bhqnkd->bhqnk', qc, k_g).astype(jnp.float32) * scale + bias_sel
        logit_sel = jnp.where(validc[None, None, :, :, None], logit_sel, -jnp.inf)
        logits = jnp.concatenate([logit_sel.reshape(B, H, Q_CHUNK, n_sel), logit_own], axis=-1)
        prob = jax.nn.softmax(logits, axis=-1)
        p_sel = prob[..., :n_sel].reshape(B, H, Q_CHUNK, k_sel, MOBA_BLOCK).astype(v.dtype)
        p_own = prob[..., n_sel:].astype(v.dtype)
        return (jnp.einsum('bhqnk,bhqnkd->bhqd', p_sel, v_g)
                + jnp.einsum('bhqk,bhkd->bhqd', p_own, v_own))

    out = lax.map(chunk_fn, (jnp.arange(n_chunks), q_c, sel_c, valid_c))
    out = out.transpose(1, 2, 0, 3, 4).reshape(B, H, s_pad, Dh)
    return out[:, :, :S]

def multiscale_pool(p):
    B, S, G, Cg = p.shape
    pf = p.astype(jnp.float32)
    cs = jnp.concatenate([jnp.zeros((B, 1, G, Cg), jnp.float32), jnp.cumsum(pf, axis=1)], axis=1)
    win = jnp.array(POOL_WINDOWS, jnp.int32)
    t = jnp.arange(S)
    lo = jnp.maximum(t[:, None] + 1 - win[None, :], 0)
    cs_lo = cs[:, lo, jnp.arange(G)[None, :], :]
    count = jnp.minimum(t[:, None] + 1, win[None, :]).astype(jnp.float32)
    mean = (cs[:, 1:] - cs_lo) / count[None, :, :, None]
    return (mean - pf).astype(p.dtype)

def causal_dwconv(u, w, b):
    C = u.shape[-1]
    y = lax.conv_general_dilated(u, w[:, None, :].astype(u.dtype), window_strides=(1,),
                                 padding=((CONV_W - 1, 0),),
                                 dimension_numbers=('NWC', 'WIO', 'NWC'),
                                 feature_group_count=C)
    return y + b

def first_inputs(seed: int = 0) -> dict:
    key = jax.random.key(seed)
    ks = jax.random.split(key, 20)
    L, D = DEPTH, D_MODEL
    nrm = lambda k, shape, s: jax.random.normal(k, shape, jnp.float32) * s
    return {
        "x": nrm(ks[0], (BATCH, SEQ, D), 1.0),
        "c": nrm(ks[1], (BATCH, D), 1.0),
        "ada_w": nrm(ks[2], (L, D, 6 * D), 0.1 * D ** -0.5),
        "ada_b": nrm(ks[3], (L, 6 * D), 0.02),
        "norm1_g": 1.0 + nrm(ks[4], (L, D), 0.05),
        "w_in": nrm(ks[5], (L, D, IN_W), D ** -0.5),
        "q_norm_g": 1.0 + nrm(ks[6], (L, HEAD_DIM), 0.05),
        "k_norm_g": 1.0 + nrm(ks[7], (L, HEAD_DIM), 0.05),
        "rel_bias": nrm(ks[8], (NUM_BUCKETS, ATTN_HEADS), 0.5),
        "pool_w": nrm(ks[9], (L, POOL_GROUPS, POOL_GROUP_W, POOL_GROUP_W), POOL_GROUP_W ** -0.5),
        "pool_scale": 1.0 + nrm(ks[10], (L, POOL_W), 0.1),
        "w_branch_attn": nrm(ks[11], (L, ATTN_W, D), ATTN_W ** -0.5),
        "w_branch_pool": nrm(ks[12], (L, POOL_W, D), POOL_W ** -0.5),
        "w_out": nrm(ks[13], (L, D, D), D ** -0.5),
        "norm2_g": 1.0 + nrm(ks[14], (L, D), 0.05),
        "w_up": nrm(ks[15], (L, D, 2 * D_FF), D ** -0.5),
        "conv_w": nrm(ks[16], (L, CONV_W, 2 * D_FF), CONV_W ** -0.5),
        "conv_b": nrm(ks[17], (L, 2 * D_FF), 0.02),
        "w_down": nrm(ks[18], (L, D_FF, D), D_FF ** -0.5),
    }

def first_block(x, c, ada_w, ada_b, norm1_g, w_in, q_norm_g, k_norm_g, rel_bias, pool_w,
              pool_scale, w_branch_attn, w_branch_pool, w_out, norm2_g, w_up, conv_w, conv_b,
              w_down):
    B, S, D = x.shape
    split_at = [ATTN_W, 2 * ATTN_W, 3 * ATTN_W, 3 * ATTN_W + POOL_W, 3 * ATTN_W + POOL_W + D_MODEL]
    c_act = jax.nn.silu(c)
    for l in range(DEPTH):
        mod = c_act @ ada_w[l] + ada_b[l]
        shift1, scale1, gate1, shift2, scale2, gate2 = [m[:, None, :] for m in jnp.split(mod, 6, axis=-1)]

        h = rms_norm(x, norm1_g[l]) * (1 + scale1) + shift1
        z = h @ w_in[l]
        q, k, v, p, g_attn, g_pool = jnp.split(z, split_at, axis=-1)
        heads = lambda t: t.reshape(B, S, ATTN_HEADS, HEAD_DIM).transpose(0, 2, 1, 3)
        q = rms_norm(heads(q), q_norm_g[l])
        k = rms_norm(heads(k), k_norm_g[l])
        attn = moba_attention(q, k, heads(v), rel_bias)
        attn = attn.transpose(0, 2, 1, 3).reshape(B, S, ATTN_W)
        pool = multiscale_pool(p.reshape(B, S, POOL_GROUPS, POOL_GROUP_W))
        pool = jnp.einsum('bsgc,gcd->bsgd', pool, pool_w[l]).reshape(B, S, POOL_W) * pool_scale[l]
        merged = (jax.nn.sigmoid(g_attn) * (attn @ w_branch_attn[l])
                  + jax.nn.sigmoid(g_pool) * (pool @ w_branch_pool[l]))
        x = x + gate1 * (merged @ w_out[l])

        h2 = rms_norm(x, norm2_g[l]) * (1 + scale2) + shift2
        u = causal_dwconv(h2 @ w_up[l], conv_w[l], conv_b[l])
        u_g, u_v = jnp.split(u, 2, axis=-1)
        x = x + gate2 * ((jax.nn.silu(u_g) * u_v) @ w_down[l])
    return x


DEPTH_2 = 2

N_HEADS = D_MODEL // HEAD_DIM
FOX_HEADS = N_HEADS // 2
SWA_HEADS = N_HEADS - FOX_HEADS
SWA_KV_HEADS = max(1, SWA_HEADS // 4)
SWA_WINDOW = 128
Q_BLOCK = 128
DSA_HEADS = N_HEADS
DSA_KV_HEADS = max(1, DSA_HEADS // 4)
IDX_HEADS = 8
IDX_DIM = 64
DSA_TOPK_MAX = 256
N_EXPERTS = 8
TOP_K = 2
D_FF_EXPERT = 1408
ROPE_THETA = 10000.0
NORM_EPS = 1e-6
N_EVEN = (DEPTH_2 + 1) // 2
N_ODD = DEPTH_2 // 2

EVEN_SPLITS = (FOX_HEADS * HEAD_DIM, FOX_HEADS * HEAD_DIM, FOX_HEADS * HEAD_DIM, FOX_HEADS,
               SWA_HEADS * HEAD_DIM, SWA_KV_HEADS * HEAD_DIM, SWA_KV_HEADS * HEAD_DIM)
EVEN_IN = sum(EVEN_SPLITS)
ODD_SPLITS = (DSA_HEADS * HEAD_DIM, DSA_KV_HEADS * HEAD_DIM, DSA_KV_HEADS * HEAD_DIM,
              IDX_HEADS * IDX_DIM, IDX_DIM, IDX_HEADS)
ODD_IN = sum(ODD_SPLITS)


def _split(t, sizes):
    return jnp.split(t, np.cumsum(sizes)[:-1].tolist(), axis=-1)

def rms_norm_2(x, g):
    xf = x.astype(jnp.float32)
    y = xf * lax.rsqrt(jnp.mean(xf * xf, axis=-1, keepdims=True) + NORM_EPS)
    return (y * g.astype(jnp.float32)).astype(x.dtype)

def ada_modulation(c, w, b):
    mod = jax.nn.silu(c) @ w + b
    return jnp.split(mod[:, None, :], 6, axis=-1)

def rope_tables(positions, dim):
    half = dim // 2
    inv_freq = ROPE_THETA ** (-jnp.arange(half, dtype=jnp.float32) / half)
    ang = positions.astype(jnp.float32)[..., None] * inv_freq
    return jnp.cos(ang)[:, :, None, :], jnp.sin(ang)[:, :, None, :]

def apply_rope(t, cos, sin):
    half = t.shape[-1] // 2
    tf = t.astype(jnp.float32)
    t1, t2 = tf[..., :half], tf[..., half:]
    return jnp.concatenate([t1 * cos - t2 * sin, t2 * cos + t1 * sin], axis=-1).astype(t.dtype)

def swiglu(h, w_gate, w_up, w_down):
    return (jax.nn.silu(h @ w_gate) * (h @ w_up)) @ w_down

def forgetting_attention(q, k, v, log_f):
    B, S, H, D = q.shape
    cum = jnp.cumsum(log_f.astype(jnp.float32), axis=1).transpose(0, 2, 1)
    kpos = jnp.arange(S)
    scale = D ** -0.5

    def block(i):
        start = i * Q_BLOCK
        qi = lax.dynamic_slice_in_dim(q, start, Q_BLOCK, axis=1)
        ci = lax.dynamic_slice_in_dim(cum, start, Q_BLOCK, axis=2)
        s = jnp.einsum('bqhd,bkhd->bhqk', qi, k, preferred_element_type=jnp.float32) * scale
        s = s + ci[..., :, None] - cum[..., None, :]
        qpos = start + jnp.arange(Q_BLOCK)
        s = jnp.where(kpos[None, :] <= qpos[:, None], s, -jnp.inf)
        p = jax.nn.softmax(s, axis=-1)
        return jnp.einsum('bhqk,bkhd->bqhd', p.astype(v.dtype), v)

    out = lax.map(block, jnp.arange(S // Q_BLOCK))
    return jnp.moveaxis(out, 0, 1).reshape(B, S, H, D)

def sliding_window_sink_attention(q, k, v, sinks):
    B, S, H, D = q.shape
    KVH = k.shape[2]
    G = H // KVH
    W = SWA_WINDOW
    nb = S // W
    qb = q.reshape(B, nb, W, KVH, G, D)

    def band_keys(t):
        tb = t.reshape(B, nb, W, KVH, D)
        prev = jnp.concatenate([jnp.zeros_like(tb[:, :1]), tb[:, :-1]], axis=1)
        return jnp.concatenate([prev, tb], axis=2)

    kk, vv = band_keys(k), band_keys(v)
    s = jnp.einsum('bnqhgd,bnshd->bnhgqs', qb, kk, preferred_element_type=jnp.float32) * D ** -0.5
    rel = (jnp.arange(W)[:, None] + W) - jnp.arange(2 * W)[None, :]
    band = (rel >= 0) & (rel < W)
    not_pad = (jnp.arange(nb)[:, None, None] > 0) | (jnp.arange(2 * W) >= W)[None, None, :]
    valid = band[None] & not_pad
    s = jnp.where(valid[None, :, None, None], s, -jnp.inf)
    sink = sinks.astype(jnp.float32).reshape(KVH, G)[None, None, :, :, None, None]
    m = jnp.maximum(jnp.max(s, axis=-1, keepdims=True), sink)
    e = jnp.exp(s - m)
    p = e / (jnp.sum(e, axis=-1, keepdims=True) + jnp.exp(sink - m))
    out = jnp.einsum('bnhgqs,bnshd->bnqhgd', p.astype(v.dtype), vv)
    return out.reshape(B, S, H, D)

def dsa_attention(q, k, v, iq, ik, iw):
    B, S, H, D = q.shape
    KVH = k.shape[2]
    G = H // KVH
    topk = min(DSA_TOPK_MAX, S // 4)
    kpos = jnp.arange(S)
    scale = D ** -0.5
    gather = jax.vmap(lambda tb, ib: tb[ib])

    def block(i):
        start = i * Q_BLOCK
        qi = lax.dynamic_slice_in_dim(q, start, Q_BLOCK, axis=1).reshape(B, Q_BLOCK, KVH, G, D)
        iqi = lax.dynamic_slice_in_dim(iq, start, Q_BLOCK, axis=1)
        iwi = lax.dynamic_slice_in_dim(iw, start, Q_BLOCK, axis=1).astype(jnp.float32)
        qpos = start + jnp.arange(Q_BLOCK)
        logits = jnp.einsum('bqhd,bsd->bqhs', iqi, ik, preferred_element_type=jnp.float32)
        score = jnp.einsum('bqh,bqhs->bqs', iwi, jax.nn.relu(logits))
        score = jnp.where((kpos[None, :] <= qpos[:, None])[None], score, -jnp.inf)
        _, idx = lax.top_k(score, topk)
        sel_valid = idx <= qpos[None, :, None]
        ks = gather(k, idx)
        vs = gather(v, idx)
        s = jnp.einsum('bqhgd,bqthd->bhgqt', qi, ks, preferred_element_type=jnp.float32) * scale
        s = jnp.where(sel_valid[:, None, None], s, -jnp.inf)
        p = jax.nn.softmax(s, axis=-1)
        o = jnp.einsum('bhgqt,bqthd->bqhgd', p.astype(v.dtype), vs)
        return o.reshape(B, Q_BLOCK, H, D)

    out = lax.map(block, jnp.arange(S // Q_BLOCK))
    return jnp.moveaxis(out, 0, 1).reshape(B, S, H, D)

def moe_swiglu(h, router_w, router_b, w_gate, w_up, w_down):
    B, S, Dm = h.shape
    t = h.reshape(B * S, Dm)
    logits = (t @ router_w).astype(jnp.float32) + router_b.astype(jnp.float32)
    top_vals, top_idx = lax.top_k(logits, TOP_K)
    gates = jax.nn.softmax(top_vals, axis=-1)
    combine = jnp.sum(jax.nn.one_hot(top_idx, N_EXPERTS, dtype=jnp.float32) * gates[..., None], axis=1)
    combine = combine.astype(h.dtype)
    out = jnp.zeros_like(t)
    for e in range(N_EXPERTS):
        out = out + combine[:, e:e + 1] * swiglu(t, w_gate[e], w_up[e], w_down[e])
    return out.reshape(B, S, Dm)

def even_layer(x, c, cos, sin, ada_w, ada_b, norm_mix, norm_ffn, w_in, forget_b, sinks, w_out,
               ffn_gate, ffn_up, ffn_down):
    B, S, _ = x.shape
    sh_m, sc_m, g_m, sh_f, sc_f, g_f = ada_modulation(c, ada_w, ada_b)
    h = rms_norm_2(x, norm_mix) * (1 + sc_m) + sh_m
    fq, fk, fv, fgl, sq, sk, sv = _split(h @ w_in, EVEN_SPLITS)
    heads = lambda t, n: t.reshape(B, S, n, HEAD_DIM)
    log_f = jax.nn.log_sigmoid((fgl + forget_b).astype(jnp.float32))
    o_fox = forgetting_attention(heads(fq, FOX_HEADS), heads(fk, FOX_HEADS), heads(fv, FOX_HEADS), log_f)
    o_swa = sliding_window_sink_attention(apply_rope(heads(sq, SWA_HEADS), cos, sin),
                                          apply_rope(heads(sk, SWA_KV_HEADS), cos, sin),
                                          heads(sv, SWA_KV_HEADS), sinks)
    mix = jnp.concatenate([o_fox.reshape(B, S, -1), o_swa.reshape(B, S, -1)], axis=-1) @ w_out
    x = x + g_m * mix
    h = rms_norm_2(x, norm_ffn) * (1 + sc_f) + sh_f
    return x + g_f * swiglu(h, ffn_gate, ffn_up, ffn_down)

def odd_layer(x, c, cos, sin, ada_w, ada_b, norm_mix, norm_ffn, w_in, w_out,
              router_w, router_b, exp_gate, exp_up, exp_down):
    B, S, _ = x.shape
    sh_m, sc_m, g_m, sh_f, sc_f, g_f = ada_modulation(c, ada_w, ada_b)
    h = rms_norm_2(x, norm_mix) * (1 + sc_m) + sh_m
    q, k, v, iq, ik, iw = _split(h @ w_in, ODD_SPLITS)
    q = apply_rope(q.reshape(B, S, DSA_HEADS, HEAD_DIM), cos, sin)
    k = apply_rope(k.reshape(B, S, DSA_KV_HEADS, HEAD_DIM), cos, sin)
    v = v.reshape(B, S, DSA_KV_HEADS, HEAD_DIM)
    iq = apply_rope(iq.reshape(B, S, IDX_HEADS, IDX_DIM), cos, sin)
    ik = apply_rope(ik.reshape(B, S, 1, IDX_DIM), cos, sin)[:, :, 0]
    iw = iw * (IDX_HEADS ** -0.5 * IDX_DIM ** -0.5)
    o = dsa_attention(q, k, v, iq, ik, iw)
    x = x + g_m * (o.reshape(B, S, -1) @ w_out)
    h = rms_norm_2(x, norm_ffn) * (1 + sc_f) + sh_f
    return x + g_f * moe_swiglu(h, router_w, router_b, exp_gate, exp_up, exp_down)

def second_inputs(seed: int = 0) -> dict:
    key = jax.random.key(seed)
    ks = iter(jax.random.split(key, 40))
    D = D_MODEL

    def nrm(shape, s):
        return jax.random.normal(next(ks), shape, jnp.float32) * s

    x = nrm((BATCH, SEQ, D), 1.0)
    c = nrm((BATCH, D), 1.0)
    offset = jax.random.randint(next(ks), (BATCH, 1), 0, 4096, dtype=jnp.int32)
    positions = offset + jnp.arange(SEQ, dtype=jnp.int32)[None, :]
    return {
        'x': x, 'c': c, 'positions': positions,
        'e_ada_w': nrm((N_EVEN, D, 6 * D), 0.5 * D ** -0.5),
        'e_ada_b': nrm((N_EVEN, 6 * D), 0.02),
        'e_norm_mix': 1.0 + nrm((N_EVEN, D), 0.05),
        'e_norm_ffn': 1.0 + nrm((N_EVEN, D), 0.05),
        'e_w_in': nrm((N_EVEN, D, EVEN_IN), D ** -0.5),
        'e_forget_b': 3.0 + nrm((N_EVEN, FOX_HEADS), 1.0),
        'e_sinks': nrm((N_EVEN, SWA_HEADS), 1.0),
        'e_w_out': nrm((N_EVEN, D, D), D ** -0.5),
        'e_ffn_gate': nrm((N_EVEN, D, D_FF), D ** -0.5),
        'e_ffn_up': nrm((N_EVEN, D, D_FF), D ** -0.5),
        'e_ffn_down': nrm((N_EVEN, D_FF, D), D_FF ** -0.5),
        'o_ada_w': nrm((N_ODD, D, 6 * D), 0.5 * D ** -0.5),
        'o_ada_b': nrm((N_ODD, 6 * D), 0.02),
        'o_norm_mix': 1.0 + nrm((N_ODD, D), 0.05),
        'o_norm_ffn': 1.0 + nrm((N_ODD, D), 0.05),
        'o_w_in': nrm((N_ODD, D, ODD_IN), D ** -0.5),
        'o_w_out': nrm((N_ODD, D, D), D ** -0.5),
        'o_router_w': nrm((N_ODD, D, N_EXPERTS), D ** -0.5),
        'o_router_b': nrm((N_ODD, N_EXPERTS), 0.01),
        'o_exp_gate': nrm((N_ODD, N_EXPERTS, D, D_FF_EXPERT), D ** -0.5),
        'o_exp_up': nrm((N_ODD, N_EXPERTS, D, D_FF_EXPERT), D ** -0.5),
        'o_exp_down': nrm((N_ODD, N_EXPERTS, D_FF_EXPERT, D), D_FF_EXPERT ** -0.5),
        'final_norm': 1.0 + nrm((D,), 0.05),
    }

def second_block(x, c, positions,
              e_ada_w, e_ada_b, e_norm_mix, e_norm_ffn, e_w_in, e_forget_b, e_sinks, e_w_out,
              e_ffn_gate, e_ffn_up, e_ffn_down,
              o_ada_w, o_ada_b, o_norm_mix, o_norm_ffn, o_w_in, o_w_out,
              o_router_w, o_router_b, o_exp_gate, o_exp_up, o_exp_down,
              final_norm):
    cos, sin = rope_tables(positions, HEAD_DIM)
    for layer in range(DEPTH_2):
        i = layer // 2
        if layer % 2 == 0:
            x = even_layer(x, c, cos, sin, e_ada_w[i], e_ada_b[i], e_norm_mix[i], e_norm_ffn[i],
                           e_w_in[i], e_forget_b[i], e_sinks[i], e_w_out[i],
                           e_ffn_gate[i], e_ffn_up[i], e_ffn_down[i])
        else:
            x = odd_layer(x, c, cos, sin, o_ada_w[i], o_ada_b[i], o_norm_mix[i], o_norm_ffn[i],
                          o_w_in[i], o_w_out[i], o_router_w[i], o_router_b[i],
                          o_exp_gate[i], o_exp_up[i], o_exp_down[i])
    return rms_norm_2(x, final_norm)


def setup_inputs(seed=0):
    out = dict(first_inputs(seed))
    for name, value in second_inputs(seed + 1).items():
        if name != "x":
            out[name + "_2"] = value
    return out


def reference(
    x, c, ada_w, ada_b, norm1_g, w_in, q_norm_g, k_norm_g, rel_bias, pool_w, pool_scale,
    w_branch_attn, w_branch_pool, w_out, norm2_g, w_up, conv_w, conv_b, w_down, c_2,
    positions_2, e_ada_w_2, e_ada_b_2, e_norm_mix_2, e_norm_ffn_2, e_w_in_2, e_forget_b_2,
    e_sinks_2, e_w_out_2, e_ffn_gate_2, e_ffn_up_2, e_ffn_down_2, o_ada_w_2, o_ada_b_2,
    o_norm_mix_2, o_norm_ffn_2, o_w_in_2, o_w_out_2, o_router_w_2, o_router_b_2, o_exp_gate_2,
    o_exp_up_2, o_exp_down_2, final_norm_2,
):
    x = first_block(
        x, c, ada_w, ada_b, norm1_g, w_in, q_norm_g, k_norm_g, rel_bias, pool_w, pool_scale,
        w_branch_attn, w_branch_pool, w_out, norm2_g, w_up, conv_w, conv_b, w_down,
    )
    return second_block(
        x, c_2, positions_2, e_ada_w_2, e_ada_b_2, e_norm_mix_2, e_norm_ffn_2, e_w_in_2,
        e_forget_b_2, e_sinks_2, e_w_out_2, e_ffn_gate_2, e_ffn_up_2, e_ffn_down_2, o_ada_w_2,
        o_ada_b_2, o_norm_mix_2, o_norm_ffn_2, o_w_in_2, o_w_out_2, o_router_w_2, o_router_b_2,
        o_exp_gate_2, o_exp_up_2, o_exp_down_2, final_norm_2,
    )


_drawn_inputs = setup_inputs


def setup_inputs(seed=0):
    import zlib

    import numpy as np

    out = dict(_drawn_inputs(seed))
    spreads = {}
    factors = {'ada_b': 2.79,
     'norm1_g': 8.0,
     'q_norm_g': 8.0,
     'k_norm_g': 8.0,
     'rel_bias': 7.348,
     'pool_scale': 8.0,
     'w_branch_attn': 4.063,
     'norm2_g': 7.323,
     'conv_b': 8.0,
     'e_norm_mix_2': 4.575,
     'e_norm_ffn_2': 2.937,
     'e_sinks_2': 19.398,
     'o_norm_mix_2': 3.042,
     'o_router_b_2': 55.936,
     'o_norm_ffn_2': 8.0}
    for name, (base, spread) in spreads.items():
        noise = np.random.default_rng([zlib.crc32(name.encode()), seed]).standard_normal(out[name].shape)
        drawn = base * np.exp(spread * noise) if base else spread * noise
        out[name] = __import__('jax').numpy.asarray(drawn.astype(out[name].dtype))
    for name, factor in factors.items():
        out[name] = (out[name] * factor).astype(out[name].dtype)
    return out
```

```python
from contextlib import ExitStack

import numpy as np

import concourse.bass as bass
from concourse import mybir

F32 = mybir.dt.float32
BF16 = mybir.dt.bfloat16
I32 = mybir.dt.int32
ACT = mybir.ActivationFunctionType
ALU = mybir.AluOpType
AX = mybir.AxisListType.X

P = 128
D = 1024
T = 256
KC = D // P
HALF = T // 2
TRI = HALF + T
HD = 64
SLOT = 1024
RING = 24
FC = 2816 // P
BODY = RING // 3
TURNS = FC // BODY
EXPERTS = 8
EF = 1408 // P
MSLOTS = 3 * EF
CAP = 96
EXTRA = (2 * T) // (CAP + 1)
NTAB = EXPERTS + EXTRA + 1
BIG = 1.0e30
TAKEN = -3.0e38
EPS = 1e-6
SCALE = HD ** -0.5
MAGIC = 12582912.0
TWO_PI_PARTS = (6.28125, 0.0019350051879882812, 3.0198999e-07)
PI_CLAMP = 3.1415925

COLS = {}
for _name, _n in (("norm1_g", 8), ("norm2_g", 8), ("e_norm_mix", 8), ("e_norm_ffn", 8), ("o_norm_mix", 8),
                  ("o_norm_ffn", 8), ("final_norm", 8), ("ada_b", 48), ("e_ada_b", 48), ("o_ada_b", 48),
                  ("pool_scale", 4), ("q_norm_g", 1), ("k_norm_g", 1), ("conv", 8 * FC), ("c", 16),
                  ("inv_freq", 1), ("rows", 24), ("fgl", 64), ("iw", 64), ("router", 64)):
    COLS[_name] = (sum(n for _, n in COLS.values()), _n)
NCOLS = sum(n for _, n in COLS.values())
NORM_GAINS = ("norm1_g", "norm2_g", "e_norm_mix", "e_norm_ffn", "o_norm_mix", "o_norm_ffn", "final_norm")

MATS = {}
for _name, _n in (("ident", 128), ("heads", 128), ("rotate", 128), ("causal", TRI), ("band", TRI),
                  ("upto", 2 * T), ("iota", CAP), ("small", 64)):
    MATS[_name] = (sum(n for _, n in MATS.values()), _n)
NMATS = sum(n for _, n in MATS.values())


class Unit:

    def __init__(self, bank, nth, pos, done):
        self.bank, self.nth, self.pos, self.done = bank, nth, pos, done


def plan_units(slot_used, aux_done):
    units = {}
    at = {"bank": 0, "nth": [0, 0], "pos": 16, "aux": 0}

    def add(name, slots=0, release=True):
        pos, bank = at["pos"], at["bank"]
        if slots and release:
            last = pos + slots - 1
            done = (slot_used[last % RING], last // RING + 1)
            at["pos"] += slots
        else:
            at["aux"] += 1
            done = (aux_done, at["aux"])
        units[name] = Unit(bank, at["nth"][bank], pos, done)
        at["nth"][bank] += 1
        at["bank"] = 1 - bank

    def loop(name):
        units[name] = Unit(0, tuple(at["nth"]), at["pos"], at["aux"])
        at["nth"] = [n + FC // 2 for n in at["nth"]]
        at["bank"] = 0
        at["pos"] += 3 * FC

    def add_all(name, n, slots=1):
        for c in range(n):
            add((name, c), slots)

    add_all("t5", 8, 0)
    add(("stat", 0))
    add_all("q", 4)
    add(("qkstat", 0))
    add(("k", 0), 1)
    add(("k", 1), 1)
    add(("qkstat", 1))
    add(("k", 2), 1)
    add(("k", 3), 1)
    add(("qkstat", 2))
    add(("v", 0), 4, release=False)
    add(("v", 1), 4)
    add(("qkstat", 3))
    add(("p", 0), 4, release=False)
    add(("p", 1), 4)
    add_all("pool", 2, 0)
    add_all("poolw", 2, 0)
    add_all("ga", 8)
    add_all("gp", 8)
    add_all("br", 8)
    add_all("wo", 8)
    add(("stat", 1))
    loop("ffn1")
    add(("stat", 2))
    add("fgl")
    add_all("fq", 4)
    add_all("fk", 4)
    add("cum")
    add(("fv", 0), 4, release=False)
    add(("fv", 1), 4)
    add(("sq", 0), 1)
    for c in range(1, 4):
        add(("sq", c), 1)
        add(("rot", c - 1))
    add(("sk", 0), 1)
    add(("rot", 3))
    add("sv", 1)
    add(("rot", 4))
    add_all("eo", 8)
    add(("stat", 3))
    loop("ffn2")
    add(("stat", 4))
    add("iw")
    add(("ik", 0), 1)
    for c in range(4):
        add(("iq", c), 1)
        add(("rot", 5 + c))
    add(("dk", 0), 1)
    add(("rot", 9))
    add(("dk", 1), 1)
    add(("rot", 10))
    add("dv", 2)
    add(("rot", 11))
    add(("dq", 0), 1)
    for c in range(1, 8):
        add(("dq", c), 1)
        add(("rot", 11 + c))
    add(("rot", 19))
    add_all("oo", 8)
    add(("stat", 5))
    add("router")
    add("ranks")
    add_all("htok", 4, 0)
    add_all("gather", 2, 0)
    units["moe"] = Unit(0, tuple(at["nth"]), at["pos"], at["aux"])
    add(("stat", 6))
    return units


def norm_scale_source(r):
    layer, ffn = divmod(r, 2)
    return ((3 * layer + 1, 8), (3 * layer + 2, 0)) if ffn else ((3 * layer, 0), (3 * layer, 8))


def program(nc, xT, cols_d, mats_d, pos_d, onehot_d, relb_d, sel_d, poolA_d, poolw_d, stream, ada1, ada2, ada3,
            experts, out):
    ctx = ExitStack()
    with ctx:
        def sb(name, shape, dt=F32):
            return ctx.enter_context(nc.sbuf_tensor(name, shape, dt))

        def sem(name):
            return ctx.enter_context(nc.semaphore(name))

        ring = sb("ring", [P, RING, SLOT])
        x = sb("x", [P, KC, T])
        h = sb("h", [P, KC, T])
        side = sb("side", [P, 6, SLOT])
        arena = sb("arena", [P, 12288])
        cols = sb("vectors", [P, NCOLS])
        mats = sb("constants", [P, NMATS])
        ones = sb("ones", [P, P])
        zeros = sb("zeros", [1, 512], BF16)
        cos = sb("cos", [P, T])
        sin = sb("sin", [P, T])
        mod = sb("mod", [P, 9, 16])
        avec = sb("avec", [P, 7, 8])
        ghalf = sb("ghalf", [P, 8])
        cact = sb("cact", [P, 16])
        negsink = sb("negsink", [P, 8])
        half_pi = sb("half_pi", [P, 1])
        var = sb("var", [P, 512])
        rstd = var[:, T:2 * T]
        logit = sb("logit", [P, 3, TRI])
        probT = sb("probT", [P, 2, TRI])
        stats = sb("stats", [P, 3, 8])
        banks = ctx.enter_context(nc.psum_tensor("banks", [P, 8, 512], F32))

        def mat(name, a=0, b=None):
            at, n = MATS[name]
            return mats[:, at + a:at + (n if b is None else b)]

        def col(name, a=0, b=None):
            at, n = COLS[name]
            return cols[:, at + a:at + (n if b is None else b)]

        def region(kib, shape, parts=P):
            n = int(np.prod(shape))
            flat = arena[0:parts, int(kib * 256):int(kib * 256) + n]
            if len(shape) == 1:
                return flat
            names = "abc"[:len(shape)]
            return flat.rearrange(f"p ({' '.join(names)}) -> p {' '.join(names)}",
                                  **{names[j]: shape[j] for j in range(len(shape) - 1)})

        ada_slot = side[:, 0:4, :].rearrange("p (s a) n -> p s (a n)", s=2)
        ada_sum = side[:, 4:6, :].rearrange("p a n -> p (a n)")
        ident = mat("ident")
        causal, band = mat("causal"), mat("band")
        upto = mat("upto").rearrange("p (a t) -> p a t", a=2)

        def moe_slot(m):
            return ring[:, m, :] if m < RING else (
                side[:, m - RING, :] if m < RING + 6 else arena[:, (m - RING - 6) * SLOT:(m - RING - 5) * SLOT])

        qT, kT = region(0, [4, T]), region(4, [4, T])
        onehot, relb = region(0, [512], 33), region(2, [8, P], 33)
        v_tok, p_tok = region(8, [2, 512]), region(12, [2, 512])
        pool2 = region(12, [4, T])
        ga, gp = region(16, [8, T]), region(24, [8, T])
        t5rows = region(16, [8, 512])
        poolw, poolT = region(16, [4, P]), region(18, [4, T])
        poolA = region(24, [2, 4, T])
        bias = region(32, [8, TRI])
        oT1 = region(44, [4, T])
        qksq = region(44, [4, T])
        merged = region(0, [8, T])
        brt = region(32, [2, 2, T])
        ang, turns, posf = region(32, [T]), region(33, [T]), region(34, [T])
        posi = region(35, [T]).bitcast(I32)
        yg, yv, sg, hid = region(12, [2, T]), region(14, [2, T]), region(16, [2, T]), region(18, [2, T])
        taps = region(20, [BODY, 8])
        fqT, fkT, fv = region(0, [4, T]), region(4, [4, T]), region(8, [2, 512])
        sqT, skT, sv = region(12, [4, T]), region(16, [T]), region(17, [2, P])
        sel8 = region(18, [8, T], 8)
        lf = region(26, [4, 2, 8])
        cum8 = region(27, [2, T], 8)
        ropet = region(29, [2, T])
        oT2 = region(32, [8, T])
        dqT, dkT, dv = region(0, [8, T]), region(8, [2, T]), region(10, [2, T])
        iqT, ikT = region(12, [4, T]), region(16, [T])
        score, work, dmask = region(17, [TRI]), region(18.5, [TRI]), region(20, [TRI])
        relu = region(21.5, [2, TRI])
        iws, top8 = region(24.5, [2, 8]), region(25, [2, 8])
        htok = region(12, [2, D])
        hg = region(20, [KC, CAP])
        ehid, esg = region(23, [2, CAP]), region(24, [2, CAP])
        yT = region(25, [KC, CAP])
        y_tok = region(28, [D], CAP)
        pickT = region(32, [T], CAP)
        pick, cpick = region(33, [2, CAP]), region(34, [2, CAP])
        rt = region(35, [1024])
        tab = region(39, [NTAB, 4])
        cur = region(39.5, [4])
        ints = region(40, [NTAB + 1]).bitcast(I32)

        slot_full = [sem(f"slot_full{s}") for s in range(MSLOTS)]
        slot_used = [sem(f"slot_used{s}") for s in range(MSLOTS)]
        ada_full = [sem(f"ada_full{s}") for s in range(2)]
        x_in, cols_in, mats_in, pos_in, onehot_in = (sem(n) for n in ("x_in", "cols_in", "mats_in", "pos_in", "onehot_in"))
        t5_stored, bias_in, pool_in, sel_in, out_stored = (sem(n) for n in ("t5_stored", "bias_in", "pool_in", "sel_in", "out_stored"))
        consts_set = sem("consts_set")
        aux_done = sem("aux_done")
        freed = [sem("freed0"), sem("freed1")]
        s_cact, s_rope_dve, s_rope_act = sem("s_cact"), sem("s_rope_dve"), sem("s_rope_act")
        s_ada, s_colsum, s_mod, s_avec = sem("s_ada"), sem("s_colsum"), sem("s_mod"), sem("s_avec")
        s_sq, s_var, s_rstd, s_xn, s_h = sem("s_sq"), sem("s_var"), sem("s_rstd"), sem("s_xn"), sem("s_h")
        s_qksq, s_qkvar, s_qkstd, s_qk = sem("s_qksq"), sem("s_qkvar"), sem("s_qkstd"), sem("s_qk")
        s_score, s_logit, s_max, s_exp, s_rsum, s_prob = (sem(n) for n in ("s_score", "s_logit", "s_max", "s_exp", "s_rsum", "s_prob"))
        s_tr, s_pt, s_pv, s_o = (sem(n) for n in ("s_tr", "s_pt", "s_pv", "s_o"))
        s_gate, s_merged = sem("s_gate"), sem("s_merged")
        s_taps_in, s_conv, s_tap, s_silu, s_acc, s_x = (sem(n) for n in ("s_taps_in", "s_conv", "s_tap", "s_silu", "s_acc", "s_x"))
        s_forget, s_cum8 = sem("s_forget"), sem("s_cum8")
        s_rot, s_rope = sem("s_rot"), sem("s_rope")
        s_iscore, s_relu, s_isum, s_topk, s_dmask = (sem(n) for n in ("s_iscore", "s_relu", "s_isum", "s_topk", "s_dmask"))
        s_route, s_routed, s_gexp, s_pick, s_cpick, s_cur = (sem(n) for n in ("s_route", "s_routed", "s_gexp", "s_pick", "s_cpick", "s_cur"))
        s_yT_act, s_yT_dve, s_scatter, s_init = (sem(n) for n in ("s_yT_act", "s_yT_dve", "s_scatter", "s_init"))
        s_final, s_pool = sem("s_final"), sem("s_pool")

        U = plan_units(slot_used, aux_done)
        scratch = nc.dram_tensor("bias_rows", (8 * P * 512,), F32, kind="Internal").ap()

        def taken(u):
            return freed[u.bank], u.nth + 1

        def bank(u, a=0, b=512, parts=P):
            return banks[0:parts, u.bank, a:b]

        def fills(pos):
            return pos // RING + 1

        class Heads:
            pass

        def heads_of(n0, count, kind):
            found = []
            for i in range(count):
                a = Heads()
                a.n = n0 + i
                a.chunk, a.half = i // 2, i % 2
                a.kind = kind
                rows = slice(64 * a.half, 64 * a.half + 64)
                if kind == "moba":
                    a.q, a.k, a.v = qT[rows, a.chunk], kT[rows, a.chunk], v_tok
                    a.vcol, a.bias, a.out = 64 * i, bias[:, i, :], oT1[:, a.chunk]
                elif kind == "fox":
                    a.q, a.k, a.v = fqT[rows, a.chunk], fkT[rows, a.chunk], fv
                    a.vcol, a.bias, a.out = 64 * i, causal, oT2[:, a.chunk]
                elif kind == "swa":
                    a.q, a.k, a.v = sqT[rows, a.chunk], skT[rows, :], sv
                    a.vcol, a.bias, a.out = 64 * a.half, band, oT2[:, 4 + a.chunk]
                    a.sink = a.chunk + 4 * a.half
                else:
                    a.q, a.k, a.v = dqT[rows, a.chunk], dkT[rows, a.chunk // 4], dv
                    a.vcol, a.bias, a.out = 128 * (a.chunk // 4) + 64 * a.half, dmask, dqT[:, a.chunk]
                a.i = i
                found.append(a)
            return found

        first_heads = heads_of(0, 8, "moba")
        even_heads = heads_of(8, 8, "fox") + heads_of(16, 8, "swa")
        odd_heads = heads_of(24, 16, "dsa")
        LAG = 2

        def max_count(n, j, sink):
            return 2 * n + min(max(n - 16, 0), 8) + (3 if sink else j + 1)

        def exp_count(n):
            return 2 * n + 2 + min(max(n - 15, 0), 8)

        def rsum_count(n):
            return n + 1 + min(max(n - 15, 0), 8)

        def x_ready(m, c):
            if m % 2:
                return s_x, 8 * (m // 2) + c + 1
            return taken(U[("wo", "eo", "oo")[m // 2], c])

        block = ctx.enter_context(nc.Block())

        @block.sync
        def _(sp):
            sp.dma_start(cols[:, :], cols_d).then_inc(cols_in, 16)
            sp.dma_start(x[:, :, :], xT).then_inc(x_in, 16)
            for s in range(RING):
                sp.dma_start(ring[:, s, :], stream[s]).then_inc(slot_full[s], 16)
                if s == 3:
                    sp.dma_start(mats[:, :], mats_d).then_inc(mats_in, 16)
            total = U["moe"].pos
            whole = total // RING
            with sp.Fori(1, whole) as t:
                for s in range(RING):
                    sp.wait_ge(slot_used[s], t)
                    sp.dma_start(ring[:, s, :],
                                 stream[bass.ds(t * RING + s, 1)].rearrange("a p n -> p (a n)")).then_inc(slot_full[s], 16)
            for pos in range(whole * RING, total):
                s = pos % RING
                sp.wait_ge(slot_used[s], whole)
                sp.dma_start(ring[:, s, :], stream[pos]).then_inc(slot_full[s], 16)
            before = [len(range(s, total, RING)) if s < RING else 0 for s in range(MSLOTS)]
            for m in range(MSLOTS):
                if m < RING:
                    sp.wait_ge(slot_used[m], before[m])
                elif m == RING:
                    sp.wait_ge(s_mod, 9)
                elif m == RING + 6:
                    sp.wait_ge(s_o, 20)
                    sp.wait_ge(U["oo", 7].done[0], U["oo", 7].done[1])
                sp.dma_start(moe_slot(m), experts[m]).then_inc(slot_full[m], 16)
            sp.wait_ge(s_routed, 1)
            passes = sp.value_load(ints[0:1, NTAB:NTAB + 1], min_val=EXPERTS, max_val=EXPERTS + EXTRA)
            with sp.Fori(1, passes) as p:
                expert = sp.value_load(ints[0:1, bass.ds(p, 1)], min_val=0, max_val=EXPERTS - 1)
                for m in range(MSLOTS):
                    sp.wait_ge(slot_used[m], before[m] + p)
                    sp.dma_start(moe_slot(m),
                                 experts[bass.ds(expert * MSLOTS + m, 1)].rearrange("a p n -> p (a n)")).then_inc(slot_full[m], 16)
            for c in range(0, KC, 2):
                sp.wait_ge(s_final, c + 2)
                sp.dma_start(out[:, c:c + 2, :], h[:, c:c + 2, :]).then_inc(out_stored, 16)
            sp.wait_ge(out_stored, 64)

        @block.gpsimd
        def _(pool):
            pool.memset(ones[:, :], 1.0).then_inc(consts_set, 1)
            pool.memset(zeros[:, :], 0.0).then_inc(consts_set, 1)
            pool.dma_start(onehot, onehot_d).then_inc(onehot_in, 16)
            pool.dma_start(relb, relb_d).then_inc(onehot_in, 16)
            pool.dma_start(posi, pos_d).then_inc(pos_in, 16)
            pool.wait_ge(*taken(U["t5", 7]))
            pool.wait_ge(*taken(U["t5", 6]))
            pool.wait_ge(slot_full[15], 16)
            pool.dma_start(scratch.rearrange("(h p n) -> p h n", h=8, n=512), t5rows).then_inc(t5_stored, 16)
            pool.wait_ge(t5_stored, 16)
            pool.wait_ge(s_rope_act, 3)
            pool.dma_start(bias[:, :, 0:HALF],
                           bass.AP(scratch.tensor, 255, [[511, P], [P * 512, 8], [1, HALF]])).then_inc(bias_in, 16)
            pool.dma_start(bias[:, :, HALF:TRI],
                           bass.AP(scratch.tensor, 127, [[511, P], [P * 512, 8], [1, T]])).then_inc(bias_in, 16)
            pool.dma_start(poolA, poolA_d).then_inc(pool_in, 16)
            pool.dma_start(poolw, poolw_d).then_inc(pool_in, 16)

            def ada_load(source, kc, third, v, i=0):
                if not (isinstance(i, int) and v + 8 * i < 2):
                    pool.wait_ge(s_ada, 2 * v - 2 + 16 * i)
                pool.dma_start(ada_slot[:, v % 2, :],
                               source[kc * P:(kc + 1) * P, bass.ds(third * 2 * SLOT, 2 * SLOT)]).then_inc(ada_full[v % 2], 16)

            for v in range(16):
                ada_load(ada1, v % 8, 1 + v // 8, v)
            for n, source in ((0, ada2), (1, ada3)):
                with pool.Fori(0, 3) as third:
                    for kc in range(KC):
                        ada_load(source, kc, third, 16 + 24 * n + kc, third)
                if n == 0:
                    pool.wait_ge(s_h, 24)
                    pool.dma_start(sel8, sel_d).then_inc(sel_in, 16)

        @block.tensor
        def _(pe):
            def begin(u):
                if u.nth:
                    pe.wait_ge(freed[u.bank], u.nth)

            def slot_in(pos):
                pe.wait_ge(slot_full[pos % RING], 16 * fills(pos))

            def project(u, moving=h, k0=0, kn=KC, a=0):
                s = u.pos % RING
                slot_in(u.pos)
                for kc in range(kn):
                    last = pe.matmul(bank(u, a, a + T), ring[:, s, (k0 + kc) * P:(k0 + kc + 1) * P], moving[:, kc, :],
                                     start=(kc == 0), stop=(kc == kn - 1))
                return last

            def feature_units(name, n, moving=h):
                for c in range(n):
                    u = U[name, c]
                    begin(u)
                    project(u, moving).then_inc(slot_used[u.pos % RING], 1)

            def one(name, moving=h):
                u = U[name]
                begin(u)
                project(u, moving).then_inc(slot_used[u.pos % RING], 1)

            def token_unit(u, tile, slots, width, at=0, release=True, do_begin=True):
                if do_begin:
                    begin(u)
                per = KC // slots
                for kc in range(KC):
                    s = (u.pos + kc // per) % RING
                    if kc % per == 0:
                        slot_in(u.pos + kc // per)
                    last = pe.matmul(bank(u, at, at + width), h[:, kc, tile * P:(tile + 1) * P],
                                     ring[:, s, (kc % per) * width:(kc % per + 1) * width],
                                     start=(kc == 0), stop=(kc == KC - 1))
                    if release and kc % per == per - 1:
                        last.then_inc(slot_used[s], 1)
                return last

            def small_tokens(u, name, width=8):
                begin(u)
                for tile in range(2):
                    for kc in range(KC):
                        last = pe.matmul(bank(u, tile * width, (tile + 1) * width), h[:, kc, tile * P:(tile + 1) * P],
                                         col(name, kc * width, (kc + 1) * width), start=(kc == 0), stop=(kc == KC - 1))
                last.then_inc(aux_done, 1)

            def norm_sum(r, u=None):
                u = u or U["stat", r]
                begin(u)
                for c in range(KC):
                    pe.wait_ge(s_sq, 8 * r + c + 1)
                    last = pe.matmul(bank(u, 0, T), ones[:, :], h[:, c, :], start=(c == 0), stop=(c == KC - 1))
                last.then_inc(aux_done, 1)

            def colsum(third, b, i=0):
                if not isinstance(i, int) or third + i > 0:
                    pe.wait_ge(s_mod, third + i)
                    pe.wait_ge(s_ada, 16 * (third + i))
                else:
                    pe.wait_ge(slot_used[14], 1)
                    pe.wait_ge(slot_used[15], 1)
                for n in range(16):
                    last = pe.matmul(banks[:, b, n:n + 1], ada_sum[:, n * P:(n + 1) * P], ones[:, 0:1],
                                     start=True, stop=True)
                last.then_inc(s_colsum, 1)

            def rotate(r, moving, ready):
                u = U["rot", r]
                begin(u)
                pe.wait_ge(*ready)
                pe.matmul(bank(u, 0, T), mat("rotate"), moving, start=True, stop=True).then_inc(aux_done, 1)

            def scores(a):
                b = 2 + a.n % 2
                if a.n >= 2:
                    pe.wait_ge(s_logit, a.n - 1)
                fox = a.kind == "fox"
                last = None
                for lo, hi, q in ((0, HALF, a.q[:, 0:HALF]), (HALF, TRI, a.q[:, HALF:T])):
                    n = hi - lo
                    last = pe.matmul(banks[:, b, lo:hi], q, a.k[:, 0:n], start=True, stop=not fox)
                    if fox:
                        qs = slice(0, HALF) if lo == 0 else slice(HALF, T)
                        pe.matmul(banks[:, b, lo:hi], cum8[:, 0, qs], sel8[:, a.i, 0:n], start=False, stop=False)
                        last = pe.matmul(banks[:, b, lo:hi], sel8[:, a.i, 0:P], cum8[:, 1, 0:n], start=False, stop=True)
                last.then_inc(s_score, 1)

            def transposes(a):
                b = 4 + a.n % 2
                pe.wait_ge(s_prob, 2 * a.n + 2)
                if a.n >= 2:
                    pe.wait_ge(s_pt, a.n - 1)
                for j in range(3):
                    last = pe.transpose(banks[:, b, j * P:(j + 1) * P], logit[:, a.n % 3, j * P:(j + 1) * P], ident)
                last.then_inc(s_tr, 1)

            def values(a):
                rows = slice(64 * a.half, 64 * a.half + 64)
                pair = a.n // 2
                at = (pair % 2) * T
                pe.wait_ge(s_pt, a.n + 1)
                if pair >= 1 and a.half == 0:
                    pe.wait_ge(s_o, pair)
                pe.matmul(banks[rows, 6, at:at + T], a.v[:, 0, a.vcol:a.vcol + 64], probT[:, a.n % 2, 0:T],
                          start=True, stop=False)
                pe.matmul(banks[rows, 6, at + HALF:at + T], a.v[:, 1, a.vcol:a.vcol + 64], probT[:, a.n % 2, T:TRI],
                          start=False, stop=True).then_inc(s_pv, 1)

            def attend(heads, between):
                for i in range(len(heads) + LAG + 1):
                    if i < len(heads):
                        scores(heads[i])
                    for step in between.get(i, ()):
                        step()
                    if 0 <= i - LAG < len(heads):
                        transposes(heads[i - LAG])
                    if i > LAG:
                        values(heads[i - LAG - 1])

            def out_open(first):
                pe.wait_ge(consts_set, 2)
                for b in range(4, 8):
                    pe.matmul(banks[:, b, :], zeros[0:1, 0:P], zeros[0:1, :], start=True, stop=False,
                              skip_group_check=True)

            def out_close():
                for b in range(4, 8):
                    last = pe.matmul(banks[:, b, :], zeros[0:1, 0:P], zeros[0:1, :], start=False, stop=True,
                                     skip_group_check=True)
                last.then_inc(s_acc, 1)

            def ffn(name, third0):
                u0 = U[name]
                out_open(name)

                def down(i, j):
                    pos = u0.pos + 3 * j + 2
                    s = pos % RING
                    pe.wait_ge(slot_full[s], 16 * (fills(pos) + i))
                    pe.wait_ge(freed[j % 2], u0.nth[j % 2] + (BODY // 2) * i + j // 2 + 1)
                    for c in range(KC):
                        last = pe.matmul(banks[:, 4 + c // 2, (c % 2) * T:(c % 2 + 1) * T],
                                         ring[:, s, c * P:(c + 1) * P], hid[:, j % 2, :],
                                         start=False, stop=False, skip_group_check=True)
                    last.then_inc(slot_used[s], 1)

                def up(i, j):
                    b = j % 2
                    pe.wait_ge(freed[b], u0.nth[b] + (BODY // 2) * i + j // 2)
                    for r in range(2):
                        pos = u0.pos + 3 * j + r
                        s = pos % RING
                        pe.wait_ge(slot_full[s], 16 * (fills(pos) + i))
                        for kc in range(KC):
                            last = pe.matmul(banks[:, b, r * T:(r + 1) * T], ring[:, s, kc * P:(kc + 1) * P], h[:, kc, :],
                                             start=(kc == 0), stop=(kc == KC - 1))
                        last.then_inc(slot_used[s], 1)

                with pe.Fori(0, TURNS) as i:
                    for j in range(BODY):
                        up(i, j)
                        if j:
                            down(i, j - 1)
                    down(i, BODY - 1)
                    colsum(third0, 3, i)
                for j in range(FC - TURNS * BODY):
                    up(TURNS, j)
                    if j:
                        down(TURNS, j - 1)
                down(TURNS, FC - TURNS * BODY - 1)
                out_close()
                colsum(third0 + TURNS, 3)

            pe.wait_ge(onehot_in, 32)
            for i in range(8):
                u = U["t5", i]
                begin(u)
                pe.matmul(bank(u), relb[:, i, :], onehot, start=True, stop=True).then_inc(aux_done, 1)
            pe.wait_ge(consts_set, 1)
            norm_sum(0)
            colsum(0, 7)
            pe.wait_ge(s_h, 8)
            pe.wait_ge(mats_in, 16)

            def qkstat(j):
                u = U["qkstat", j]
                begin(u)
                for e in range(2):
                    c = 2 * j + e
                    pe.wait_ge(s_qksq, c + 1)
                    last = pe.matmul(bank(u, e * T, (e + 1) * T), mat("heads"), qksq[:, c % 4, :], start=True, stop=True)
                last.then_inc(aux_done, 1)

            feature_units("q", 4)
            qkstat(0)
            one(("k", 0))
            one(("k", 1))
            qkstat(1)
            one(("k", 2))
            one(("k", 3))
            qkstat(2)
            token_unit(U["v", 0], 0, 4, 512, release=False).then_inc(aux_done, 1)
            token_unit(U["v", 1], 1, 4, 512)
            qkstat(3)
            token_unit(U["p", 0], 0, 4, 512, release=False).then_inc(aux_done, 1)
            token_unit(U["p", 1], 1, 4, 512)
            pe.wait_ge(pool_in, 32)
            pe.wait_ge(*taken(U["p", 0]))
            pe.wait_ge(*taken(U["p", 1]))
            for g2 in range(2):
                u = U["pool", g2]
                begin(u)
                for e in range(2):
                    g = 2 * g2 + e
                    pe.matmul(bank(u, e * T, (e + 1) * T), p_tok[:, 0, g * P:(g + 1) * P], poolA[:, 0, g, :],
                              start=True, stop=False)
                    last = pe.matmul(bank(u, e * T + HALF, (e + 1) * T), p_tok[:, 1, g * P:(g + 1) * P],
                                     poolA[:, 1, g, HALF:T], start=False, stop=True)
                last.then_inc(aux_done, 1)
            for g2 in range(2):
                u = U["poolw", g2]
                begin(u)
                pe.wait_ge(*taken(U["pool", g2]))
                for e in range(2):
                    g = 2 * g2 + e
                    last = pe.matmul(bank(u, e * T, (e + 1) * T), poolw[:, g, :], poolT[:, g, :], start=True, stop=True)
                last.then_inc(aux_done, 1)
            pe.wait_ge(s_qk, 8)
            pe.wait_ge(*taken(U["v", 0]))
            pe.wait_ge(*taken(U["v", 1]))
            gates = [("ga", c) for c in range(8)] + [("gp", c) for c in range(8)]
            between = {i: [lambda g=g: one(g) for g in gates[2 * i:2 * i + 2]] for i in range(8)}
            between[4].append(lambda: colsum(1, 7))
            attend(first_heads, between)
            pe.wait_ge(s_o, 4)
            pe.wait_ge(*taken(U["poolw", 0]))
            pe.wait_ge(*taken(U["poolw", 1]))
            for c in range(8):
                u = U["br", c]
                begin(u)
                project(u, oT1, 0, 4, 0)
                project(u, pool2, 4, 4, T).then_inc(slot_used[u.pos % RING], 1)
            colsum(2, 7)
            pe.wait_ge(s_merged, 16)
            feature_units("wo", 8, merged)
            norm_sum(1)
            pe.wait_ge(s_h, 16)
            ffn("ffn1", 3)
            norm_sum(2)
            pe.wait_ge(s_h, 24)
            small_tokens(U["fgl"], "fgl")
            feature_units("fq", 4)
            feature_units("fk", 4)
            u = U["cum"]
            begin(u)
            pe.wait_ge(s_forget, 6)
            pe.matmul(banks[0:8, u.bank, 0:T], lf[:, 3, 0, :], upto[:, 0, :], start=True, stop=False)
            pe.matmul(banks[0:8, u.bank, HALF:T], lf[:, 3, 1, :], upto[:, 1, HALF:T], start=False, stop=True).then_inc(aux_done, 1)
            token_unit(U["fv", 0], 0, 4, 512, release=False).then_inc(aux_done, 1)
            token_unit(U["fv", 1], 1, 4, 512)
            pe.wait_ge(sel_in, 16)
            pe.wait_ge(s_cum8, 1)
            pe.wait_ge(s_mod, 6)
            for name in ("fk", 3), ("fk", 2), "cum", ("fv", 0), ("fv", 1):
                pe.wait_ge(*taken(U[name]))

            def sv_unit():
                u = U["sv"]
                token_unit(u, 0, 1, P, 0, release=False)
                token_unit(u, 1, 1, P, P, do_begin=False)

            def rot_of(r, name, c, tile):
                return lambda: rotate(r, tile, taken(U[name, c]))

            def swa_ready():
                pe.wait_ge(s_rope, 5)
                pe.wait_ge(*taken(U["sv"]))

            between = {0: [lambda: one(("sq", 0))],
                       1: [lambda: one(("sq", 1)), rot_of(0, "sq", 0, sqT[:, 0])],
                       2: [lambda: one(("sq", 2)), rot_of(1, "sq", 1, sqT[:, 1])],
                       3: [lambda: one(("sq", 3)), rot_of(2, "sq", 2, sqT[:, 2])],
                       4: [lambda: one(("sk", 0)), rot_of(3, "sq", 3, sqT[:, 3])],
                       5: [sv_unit, rot_of(4, "sk", 0, skT)],
                       7: [swa_ready]}
            attend(even_heads, between)
            pe.wait_ge(s_o, 12)
            feature_units("eo", 8, oT2)
            norm_sum(3)
            pe.wait_ge(s_h, 32)
            ffn("ffn2", 6)
            norm_sum(4)
            pe.wait_ge(s_h, 40)
            small_tokens(U["iw"], "iw")
            one(("ik", 0))
            for c in range(4):
                one(("iq", c))
                rotate(5 + c, *((ikT, taken(U["ik", 0])) if c == 0 else (iqT[:, c - 1], taken(U["iq", c - 1]))))
            one(("dk", 0))
            rotate(9, iqT[:, 3], taken(U["iq", 3]))
            one(("dk", 1))
            for m in range(8):
                pe.wait_ge(s_rope, 7 + m // 2)
                if m == 0:
                    pe.wait_ge(s_logit, 24)
                    pe.wait_ge(s_mod, 9)
                if m >= 2:
                    pe.wait_ge(s_relu, m - 1)
                rows = slice(64 * (m % 2), 64 * (m % 2) + 64)
                pe.matmul(banks[:, 2 + m % 2, 0:HALF], iqT[rows, m // 2, 0:HALF], ikT[rows, 0:HALF], start=True, stop=True)
                pe.matmul(banks[:, 2 + m % 2, HALF:TRI], iqT[rows, m // 2, HALF:T], ikT[rows, :], start=True, stop=True)\
                  .then_inc(s_iscore, 1)
            rotate(10, dkT[:, 0], taken(U["dk", 0]))
            u = U["dv"]
            token_unit(u, 0, 2, T, 0, release=False)
            token_unit(u, 1, 2, T, T, do_begin=False)
            rotate(11, dkT[:, 1], taken(U["dk", 1]))
            one(("dq", 0))

            def dq(c):
                def step():
                    if c < 8:
                        one(("dq", c))
                    rotate(11 + c, dqT[:, c - 1], taken(U["dq", c - 1]))
                return step

            for c in range(1, 4):
                dq(c)()
            pe.wait_ge(*taken(U["dv"]))
            pe.wait_ge(s_relu, 8)
            between = {}
            for c in range(4, 9):
                between[2 * (c - 4)] = between.get(2 * (c - 4), []) + [dq(c)]
            for c in range(1, 8):
                between.setdefault(2 * c - 1, []).append(lambda c=c: pe.wait_ge(s_rope, 13 + c))
            pe.wait_ge(s_rope, 13)
            attend(odd_heads, between)
            pe.wait_ge(s_o, 20)
            feature_units("oo", 8, dqT)
            norm_sum(5)
            pe.wait_ge(s_h, 48)
            small_tokens(U["router"], "router")
            u = U["ranks"]
            begin(u)
            pe.wait_ge(s_route, 9)
            picked = rt[:, 0:16].rearrange("p (a e) -> p a e", a=2)
            pe.matmul(bank(u, 0, 8), upto[:, 0, 0:HALF], picked[:, 0, :], start=True, stop=True)
            pe.matmul(bank(u, 8, 16), upto[:, 0, HALF:T], picked[:, 0, :], start=True, stop=False)
            pe.matmul(bank(u, 8, 16), upto[:, 1, HALF:T], picked[:, 1, :], start=False, stop=True)
            pe.matmul(bank(u, 16, 24), ones[:, :], picked[:, 0, :], start=True, stop=False)
            pe.matmul(bank(u, 16, 24), ones[:, :], picked[:, 1, :], start=False, stop=True).then_inc(aux_done, 1)
            for t in range(4):
                u = U["htok", t]
                begin(u)
                for j in range(4):
                    last = pe.transpose(bank(u, j * P, (j + 1) * P), h[:, 4 * (t % 2) + j, (t // 2) * P:(t // 2 + 1) * P], ident)
                last.then_inc(aux_done, 1)

            def gather(b, half):
                for j in range(4):
                    c = 4 * half + j
                    for tile in range(2):
                        last = pe.matmul(banks[:, b, j * CAP:(j + 1) * CAP], htok[:, tile, c * P:(c + 1) * P], pick[:, tile, :],
                                         start=(tile == 0), stop=(tile == 1))
                last.then_inc(aux_done, 1)

            for t in range(2, 4):
                pe.wait_ge(*taken(U["htok", t]))
            for half in range(2):
                begin(U["gather", half])
                pe.wait_ge(s_pick, 2)
                gather(U["gather", half].bank, half)
            m0 = U["moe"]
            before = [len(range(s, m0.pos, RING)) if s < RING else 0 for s in range(MSLOTS)]
            pe.wait_ge(s_routed, 1)
            passes = pe.value_load(ints[0:1, NTAB:NTAB + 1], min_val=EXPERTS, max_val=EXPERTS + EXTRA)
            out_open("moe")

            def bank_free(p, r):
                pe.wait_ge(freed[r % 2], m0.nth[r % 2] + 8 * p + r // 2)

            def y_transposes(p, r, half):
                bank_free(p, r)
                for j in range(4):
                    last = pe.transpose(banks[0:CAP, r % 2, j * P:(j + 1) * P], yT[:, 4 * half + j, :], ident)
                last.then_inc(aux_done, 1)

            def scatter():
                for c in range(KC):
                    last = pe.matmul(banks[:, 4 + c // 2, (c % 2) * T:(c % 2 + 1) * T], y_tok[:, c * P:(c + 1) * P], pickT[:, :],
                                     start=False, stop=False, skip_group_check=True)
                return last

            def expert_up(p, f):
                r = (0, 3)[f] if f < 2 else f + 3
                bank_free(p, r)
                if f == 0:
                    pe.wait_ge(freed[0], m0.nth[0] + 8 * p)
                    pe.wait_ge(freed[1], m0.nth[1] + 8 * p)
                for e in range(2):
                    m = 3 * f + e
                    pe.wait_ge(slot_full[m], 16 * (before[m] + p + 1))
                    for kc in range(KC):
                        last = pe.matmul(banks[:, r % 2, e * T:e * T + CAP], moe_slot(m)[:, kc * P:(kc + 1) * P], hg[:, kc, :],
                                         start=(kc == 0), stop=(kc == KC - 1))
                    last.then_inc(slot_used[m], 1)

            def expert_down(p, f):
                m = 3 * f + 2
                r = (0, 3)[f] if f < 2 else f + 3
                pe.wait_ge(slot_full[m], 16 * (before[m] + p + 1))
                pe.wait_ge(freed[r % 2], m0.nth[r % 2] + 8 * p + r // 2 + 1)
                if f == 0:
                    pe.wait_ge(s_yT_act, p + 1)
                    pe.wait_ge(s_yT_dve, p + 1)
                for c in range(KC):
                    last = pe.matmul(banks[:, 2 + c // 4, (c % 4) * CAP:(c % 4 + 1) * CAP], moe_slot(m)[:, c * P:(c + 1) * P],
                                     ehid[:, f % 2, :], start=(f == 0 and c % 4 == 0), stop=(f == EF - 1),
                                     skip_group_check=True)
                last.then_inc(slot_used[m], 1)

            with pe.Fori(0, passes) as p:
                expert_up(p, 0)
                pe.wait_ge(s_yT_act, p + 1)
                pe.wait_ge(s_yT_dve, p + 1)
                y_transposes(p, 1, 0)
                y_transposes(p, 2, 1)
                expert_up(p, 1)
                pe.wait_ge(freed[1], m0.nth[1] + 8 * p + 1)
                pe.wait_ge(freed[0], m0.nth[0] + 8 * p + 2)
                scatter().then_inc(s_scatter, 1)
                bank_free(p, 4)
                pe.wait_ge(s_cpick, 2 * p + 2)
                for tile in range(2):
                    last = pe.transpose(banks[0:CAP, 0, tile * P:(tile + 1) * P], cpick[:, tile, :], ident)
                last.then_inc(aux_done, 1)
                expert_down(p, 0)
                for f in range(2, EF):
                    expert_up(p, f)
                    if f == EF - 1:
                        pe.wait_ge(s_pick, 2 * p + 4)
                        for half in range(2):
                            bank_free(p, 14 + half)
                            gather(half, half)
                    expert_down(p, f - 1)
                expert_down(p, EF - 1)
            pe.wait_ge(s_yT_act, passes + 1)
            pe.wait_ge(s_yT_dve, passes + 1)
            y_transposes(passes, 0, 0)
            y_transposes(passes, 1, 1)
            pe.wait_ge(freed[0], m0.nth[0] + 8 * passes + 1)
            pe.wait_ge(freed[1], m0.nth[1] + 8 * passes + 1)
            scatter()
            out_close()
            pe.wait_ge(freed[0], m0.nth[0] + 8 * passes + 1)
            for c in range(KC):
                pe.wait_ge(s_sq, 48 + c + 1)
                last = pe.matmul(banks[:, 0, 0:T], ones[:, :], h[:, c, :], start=(c == 0), stop=(c == KC - 1))
            last.then_inc(aux_done, 1)

        @block.scalar
        def _(act):
            def take(u, out, a=0, b=512, parts=P, func=ACT.Copy, **k):
                act.wait_ge(*u.done)
                act.activation(out, bank(u, a, b, parts), func, **k).then_inc(freed[u.bank], 1)

            def squares(r):
                for c in range(KC):
                    if r == 0:
                        if c == 0:
                            act.wait_ge(x_in, 16)
                    else:
                        act.wait_ge(*x_ready(r - 1, c))
                    act.activation(h[:, c, :], x[:, c, :], ACT.Square).then_inc(s_sq, 1)

            def root(r):
                act.wait_ge(s_var, 2 * r + 2)
                act.activation(rstd, var[:, 0:T], ACT.Sqrt).then_inc(s_rstd, 1)

            def scale_shift(r):
                act.wait_ge(s_avec, r + 1)
                third, at = norm_scale_source(r)[0]
                for c in range(KC):
                    act.wait_ge(s_xn, 8 * r + c + 1)
                    act.activation(h[:, c, :], h[:, c, :], ACT.Identity, scale=avec[:, r, c:c + 1],
                                   bias=mod[:, third, at + c:at + c + 1]).then_inc(s_h, 1)

            def norm(r):
                squares(r)
                root(r)
                scale_shift(r)

            def exps(a):
                st, lg = stats[:, a.n % 3], logit[:, a.n % 3]
                sink = a.kind == "swa"
                for j, (lo, hi) in enumerate(((0, HALF), (HALF, TRI))):
                    act.wait_ge(s_max, max_count(a.n, j, sink))
                    act.activation(lg[:, lo:hi], lg[:, lo:hi], ACT.Exp, bias=st[:, j:j + 1],
                                   accum_out=st[:, 2 + j:3 + j]).then_inc(s_exp, 1)
                if sink:
                    act.activation(st[:, 6:8], st[:, 0:2], ACT.Exp,
                                   bias=col("rows", 8 + a.sink, 9 + a.sink)).then_inc(s_exp, 1)

            def attend(heads, between):
                for i in range(len(heads) + LAG + 1):
                    if i < len(heads):
                        exps(heads[i])
                    for step in between.get(i, ()):
                        step()
                    if 0 <= i - LAG < len(heads):
                        a = heads[i - LAG]
                        act.wait_ge(s_tr, a.n + 1)
                        if a.n >= 2:
                            act.wait_ge(s_pv, a.n - 1)
                        act.activation(probT[:, a.n % 2, :], banks[:, 4 + a.n % 2, 0:TRI], ACT.Copy).then_inc(s_pt, 1)
                    if i > LAG and heads[i - LAG - 1].half:
                        a = heads[i - LAG - 1]
                        at = (a.n // 2 % 2) * T
                        act.wait_ge(s_pv, a.n + 1)
                        act.activation(a.out, banks[:, 6, at:at + T], ACT.Copy).then_inc(s_o, 1)

            def ffn(name, conv, f0):
                u0 = U[name]

                def chunk(i, j):
                    b = j % 2
                    f = BODY * i + j
                    up = u0.pos + 3 * j + 1
                    act.wait_ge(slot_used[up % RING], fills(up) + i)
                    if not conv:
                        act.activation(sg[:, b, :], banks[:, b, 0:T], ACT.Silu).then_inc(s_silu, 1)
                        return
                    if j == 0:
                        act.wait_ge(s_taps_in, i + 1)
                    act.activation(yg[:, b, :], banks[:, b, 0:T], ACT.Identity, scale=taps[:, j, 2:3],
                                   bias=taps[:, j, 3:4]).then_inc(s_conv, 1)
                    act.activation(yv[:, b, :], banks[:, b, T:2 * T], ACT.Identity, scale=taps[:, j, 6:7],
                                   bias=taps[:, j, 7:8]).then_inc(s_conv, 1)
                    act.wait_ge(s_tap, 4 * f + 3)
                    act.activation(sg[:, b, :], yg[:, b, :], ACT.Silu).then_inc(s_silu, 1)

                if conv:
                    act.nop().then_inc(s_conv, 1)
                with act.Fori(0, TURNS) as i:
                    for j in range(BODY):
                        chunk(i, j)
                for j in range(FC - TURNS * BODY):
                    chunk(TURNS, j)

            act.wait_ge(cols_in, 16)
            act.activation(cact[:, :], col("c"), ACT.Silu).then_inc(s_cact, 1)
            for i in range(8):
                take(U["t5", i], t5rows[:, i, :])
            act.wait_ge(s_rope_dve, 9)
            act.activation(sin[:, :], ang, ACT.Sin).then_inc(s_rope_act, 1)
            act.activation(turns, ang, ACT.Abs).then_inc(s_rope_act, 1)
            act.wait_ge(s_rope_act, 2)
            act.wait_ge(s_rope_dve, 10)
            act.activation(cos[:, :], turns, ACT.Sin, scale=-1.0, bias=half_pi[:, :]).then_inc(s_rope_act, 1)
            norm(0)
            act.wait_ge(s_rope_act, 3)

            def take_qk(c):
                u = U[("q", "k")[c // 4], c % 4]
                act.wait_ge(*u.done)
                if c >= 4:
                    act.wait_ge(*U["qkstat", (c - 4) // 2].done)
                act.activation(qksq[:, c % 4, :], bank(u, 0, T), ACT.Square).then_inc(s_qksq, 1)
                act.activation((qT, kT)[c // 4][:, c % 4, :], bank(u, 0, T), ACT.Copy).then_inc(freed[u.bank], 1)

            def qk_root(j):
                act.wait_ge(s_qkvar, j + 1)
                act.activation(var[:, :], var[:, :], ACT.Sqrt).then_inc(s_qkstd, 1)

            for c in range(6):
                take_qk(c)
            qk_root(0)
            take_qk(6)
            take_qk(7)
            qk_root(1)
            take(U["v", 0], v_tok[:, 0, :])
            qk_root(2)
            take(U["v", 1], v_tok[:, 1, :])
            qk_root(3)
            take(U["p", 0], p_tok[:, 0, :])
            take(U["p", 1], p_tok[:, 1, :])
            for g in range(2):
                take(U["pool", g], poolT[:, 2 * g:2 * g + 2, :].rearrange("p a t -> p (a t)"))
            for g2 in range(2):
                u = U["poolw", g2]
                act.wait_ge(*u.done)
                for e in range(2):
                    g = 2 * g2 + e
                    ins = act.activation(pool2[:, g, :], bank(u, e * T, (e + 1) * T), ACT.Copy,
                                         scale=col("pool_scale", g, g + 1))
                    ins.then_inc(*((freed[u.bank], 1) if e else (s_pool, 1)))
            gates = [("ga", c) for c in range(8)] + [("gp", c) for c in range(8)]

            def take_gate(g):
                take(U[g], (ga if g[0] == "ga" else gp)[:, g[1], :], 0, T, func=ACT.Tanh, scale=0.5)

            attend(first_heads, {i: [lambda g=g: take_gate(g) for g in gates[2 * i:2 * i + 2]] for i in range(8)})
            norm(1)
            ffn("ffn1", True, 0)
            norm(2)
            act.wait_ge(s_forget, 1)
            act.wait_ge(*taken(U["fgl"]))
            flat = lf.rearrange("p a b c -> p a (b c)")
            act.activation(flat[:, 1], flat[:, 0], ACT.Abs).then_inc(s_forget, 1)
            act.wait_ge(s_forget, 2)
            act.activation(flat[:, 1], flat[:, 1], ACT.Exp, scale=-1.0).then_inc(s_forget, 1)
            act.wait_ge(s_forget, 3)
            act.activation(flat[:, 1], flat[:, 1], ACT.Ln, bias=1.0).then_inc(s_forget, 1)
            for c in range(4):
                take(U["fq", c], fqT[:, c, :], 0, T)
            for c in range(4):
                take(U["fk", c], fkT[:, c, :], 0, T)
            take(U["fv", 0], fv[:, 0, :])
            take(U["fv", 1], fv[:, 1, :])
            between = {c: [lambda c=c: take(U["sq", c], sqT[:, c, :], 0, T)] for c in range(4)}
            between[4] = [lambda: take(U["sk", 0], skT, 0, T)]
            between[5] = [lambda: take(U["sv"], sv.rearrange("p a n -> p (a n)"), 0, T)]
            attend(even_heads, between)
            norm(3)
            ffn("ffn2", False, FC)
            norm(4)
            take(U["iw"], iws.rearrange("p a n -> p (a n)"), 0, 16, scale=float(8 ** -0.5 * 64 ** -0.5))
            take(U["ik", 0], ikT, 0, T)
            for c in range(4):
                take(U["iq", c], iqT[:, c, :], 0, T)
            for c in range(2):
                take(U["dk", c], dkT[:, c, :], 0, T)
            for m in range(8):
                act.wait_ge(s_iscore, m + 1)
                if m >= 2:
                    act.wait_ge(s_isum, 2 * m - 2)
                act.activation(relu[:, m % 2, :], banks[:, 2 + m % 2, 0:TRI], ACT.Relu).then_inc(s_relu, 1)
            take(U["dv"], dv.rearrange("p a n -> p (a n)"))
            for c in range(4):
                take(U["dq", c], dqT[:, c, :], 0, T)
            attend(odd_heads, {2 * (c - 4): [lambda c=c: take(U["dq", c], dqT[:, c, :], 0, T)] for c in range(4, 8)})
            norm(5)
            act.wait_ge(s_route, 11)
            lg = rt[:, 112:128]
            act.activation(lg, lg, ACT.Exp).then_inc(s_gexp, 1)
            for t in range(4):
                take(U["htok", t], htok[:, t // 2, (t % 2) * 512:(t % 2 + 1) * 512])
            for half in range(2):
                take(U["gather", half], hg[:, 4 * half:4 * half + 4, :].rearrange("p a n -> p (a n)"), 0, 4 * CAP)
            m0 = U["moe"]
            before = [len(range(s, m0.pos, RING)) if s < RING else 0 for s in range(MSLOTS)]
            act.wait_ge(s_routed, 1)
            passes = act.value_load(ints[0:1, NTAB:NTAB + 1], min_val=EXPERTS, max_val=EXPERTS + EXTRA)
            act.wait_ge(s_init, 1)
            act.nop().then_inc(s_yT_act, 1)

            def token_major(p, b, half, aux):
                act.wait_ge(aux_done, m0.done + 5 * p + aux)
                act.activation(y_tok[:, half * 512:(half + 1) * 512], banks[0:CAP, b, :], ACT.Copy).then_inc(freed[b], 1)

            with act.Fori(0, passes) as p:
                for f in range(EF):
                    r = (0, 3)[f] if f < 2 else f + 3
                    act.wait_ge(slot_used[3 * f + 1], before[3 * f + 1] + p + 1)
                    act.activation(esg[:, f % 2, :], banks[:, r % 2, 0:CAP], ACT.Silu).then_inc(s_silu, 1)
                    if f == 0:
                        token_major(p, 1, 0, 1)
                act.wait_ge(aux_done, m0.done + 5 * p + 5)
                act.activation(hg[:, 4:8, :].rearrange("p a n -> p (a n)"), banks[:, 1, 0:4 * CAP], ACT.Copy).then_inc(freed[1], 1)
                act.wait_ge(slot_used[MSLOTS - 1], before[MSLOTS - 1] + p + 1)
                act.activation(yT[:, 0:4, :].rearrange("p a n -> p (a n)"), banks[:, 2, 0:4 * CAP], ACT.Copy).then_inc(s_yT_act, 1)
            token_major(passes, 0, 0, 1)
            squares(6)
            root(6)
            for c in range(KC):
                act.wait_ge(s_xn, 48 + c + 1)
                act.activation(h[:, c, :], h[:, c, :], ACT.Identity, scale=col("final_norm", c, c + 1)).then_inc(s_final, 1)

        @block.vector
        def _(dve):
            def norm(r, source=None, done=None):
                u = U["stat", r]
                source = source if source is not None else bank(u, 0, T)
                dve.wait_ge(*(done or u.done))
                dve.tensor_scalar(var[:, 0:T], source, 1.0 / D, EPS, ALU.mult, ALU.add).then_inc(s_var, 1)
                dve.wait_ge(s_var, 2 * r + 1)
                dve.reciprocal(var[:, 0:T], var[:, 0:T]).then_inc(s_var, 1)
                dve.wait_ge(s_rstd, r + 1)
                for c in range(KC):
                    ins = dve.tensor_tensor(h[:, c, :], x[:, c, :], rstd, ALU.mult)
                    ins.then_inc(s_xn, 1)

            def free_stat(r):
                dve.wait_ge(s_var, 2 * r + 1)
                dve.engine_nop().then_inc(freed[U["stat", r].bank], 1)

            def ada_half(third, kc, half, source, slot_ready, inc, i=0, n=None):
                layer0 = isinstance(third, int) and third < 3
                scalar = cact[:, kc:kc + 1] if layer0 else cact[:, 8 + kc:9 + kc]
                part = ada_sum[:, half * SLOT:(half + 1) * SLOT]
                dve.wait_ge(*slot_ready)
                if kc == 0:
                    if not (isinstance(third, int) and third == 0):
                        dve.wait_ge(s_colsum, third + i)
                    dve.tensor_scalar(part, source, scalar, None, ALU.mult).then_inc(*inc)
                else:
                    if n is None:
                        dve.wait_ge(slot_used[2 * kc + half - 2], 1)
                    else:
                        dve.wait_ge(s_ada, n - 1 + 16 * i)
                    dve.scalar_tensor_tensor(part, source, scalar, part, ALU.mult, ALU.add).then_inc(*inc)

            def ada_unit(third, kc, i=0):
                v = 8 * (third - 1) + kc
                for half in range(2):
                    ada_half(third, kc, half, ada_slot[:, v % 2, half * SLOT:(half + 1) * SLOT],
                             (ada_full[v % 2], 16 * (v // 2 + 1) + 64 * i), (s_ada, 1), i, 2 * v + half)

            def modulation(third, b, name, i=0):
                dve.wait_ge(s_colsum, third + 1 + i)
                n = third % 3
                if isinstance(i, int):
                    dve.tensor_tensor(mod[:, third + i, :], banks[:, b, 0:16], col(name, 16 * (n + i), 16 * (n + i) + 16), ALU.add)\
                       .then_inc(s_mod, 1)
                else:
                    at = COLS[name][0]
                    dve.tensor_tensor(mod[:, bass.ds(third + i, 1), :].rearrange("p a n -> p (a n)"), banks[:, b, 0:16],
                                      cols[:, bass.ds(at + 16 * i, 16)], ALU.add).then_inc(s_mod, 1)

            def norm_vector(r):
                third, at = norm_scale_source(r)[1]
                dve.wait_ge(s_mod, third + 1)
                dve.scalar_tensor_tensor(avec[:, r, :], mod[:, third, at:at + 8], 1.0, col(NORM_GAINS[r]),
                                         ALU.add, ALU.mult).then_inc(s_avec, 1)

            def softmax_start(a):
                st, lg = stats[:, a.n % 3], logit[:, a.n % 3]
                sink = a.kind == "swa"
                dve.wait_ge(s_score, a.n + 1)
                if a.n >= 3:
                    dve.wait_ge(s_tr, a.n - 2)
                dve.scalar_tensor_tensor(lg, banks[:, 2 + a.n % 2, 0:TRI], SCALE, a.bias, ALU.mult, ALU.add).then_inc(s_logit, 1)
                dve.wait_ge(s_logit, a.n + 1)
                for j, (lo, hi) in enumerate(((0, HALF), (HALF, TRI))):
                    dve.tensor_reduce(st[:, j:j + 1], lg[:, lo:hi], AX, ALU.max, negate=True).then_inc(s_max, 1)
                if sink:
                    dve.wait_ge(s_max, max_count(a.n, 1, False))
                    dve.tensor_scalar(st[:, 0:2], st[:, 0:2], negsink[:, a.sink:a.sink + 1], None, ALU.min).then_inc(s_max, 1)

            def softmax_end(a):
                st, lg = stats[:, a.n % 3], logit[:, a.n % 3]
                dve.wait_ge(s_exp, exp_count(a.n))
                if a.kind == "swa":
                    dve.tensor_tensor(st[:, 2:4], st[:, 2:4], st[:, 6:8], ALU.add).then_inc(s_rsum, 1)
                    dve.wait_ge(s_rsum, rsum_count(a.n) - 1)
                dve.reciprocal(st[:, 4:6], st[:, 2:4]).then_inc(s_rsum, 1)
                dve.wait_ge(s_rsum, rsum_count(a.n))
                for j, (lo, hi) in enumerate(((0, HALF), (HALF, TRI))):
                    dve.tensor_scalar(lg[:, lo:hi], lg[:, lo:hi], st[:, 4 + j:5 + j], None, ALU.mult).then_inc(s_prob, 1)

            def attend(heads, between):
                for i in range(len(heads) + 1):
                    if i < len(heads):
                        softmax_start(heads[i])
                    if i >= 1:
                        softmax_end(heads[i - 1])
                    for step in between.get(i, ()):
                        step()

            def rope(r, tile, raw):
                u = U["rot", r]
                dve.wait_ge(*u.done)
                dve.tensor_tensor(ropet[:, r % 2, :], bank(u, 0, T), sin[:, :], ALU.mult).then_inc(freed[u.bank], 1)
                dve.wait_ge(*taken(U[raw]))
                dve.tensor_tensor(tile, tile, cos[:, :], ALU.mult).then_inc(s_rot, 1)
                dve.wait_ge(s_rot, r + 1)
                dve.wait_ge(*taken(u))
                dve.tensor_tensor(tile, tile, ropet[:, r % 2, :], ALU.add).then_inc(s_rope, 1)

            def residual_units(name, gate):
                for c in range(KC):
                    u = U[name, c]
                    dve.wait_ge(*u.done)
                    dve.scalar_tensor_tensor(x[:, c, :], bank(u, 0, T), gate[:, c:c + 1], x[:, c, :], ALU.mult, ALU.add)\
                       .then_inc(freed[u.bank], 1)

            def residual_acc(layer):
                dve.wait_ge(s_acc, layer + 1)
                for c in range(KC):
                    dve.scalar_tensor_tensor(x[:, c, :], banks[:, 4 + c // 2, (c % 2) * T:(c % 2 + 1) * T],
                                             mod[:, 3 * layer + 2, 8 + c:9 + c], x[:, c, :], ALU.mult, ALU.add).then_inc(s_x, 1)

            def ffn(name, conv, third0, ada_b):
                u0 = U[name]
                f0 = 0 if conv else FC

                def chunk(i, j, units):
                    b = j % 2
                    f = BODY * i + j
                    up = u0.pos + 3 * j + 1
                    if conv:
                        if j == 0:
                            if not (isinstance(i, int) and i == 0):
                                dve.wait_ge(s_conv, 2 * BODY * i + 1)
                            at = COLS["conv"][0]
                            n = 8 * BODY if not isinstance(i, int) else 8 * (FC - TURNS * BODY)
                            source = cols[:, bass.ds(at + 8 * BODY * i, n)]
                            dve.tensor_copy(taps.rearrange("p a b -> p (a b)")[:, 0:n], source).then_inc(s_taps_in, 1)
                            dve.wait_ge(s_taps_in, i + 1)
                        for tap in (1, 0):
                            for e, y in ((0, yg), (1, yv)):
                                if tap == 1:
                                    dve.wait_ge(s_conv, 2 * f + 3)
                                else:
                                    dve.wait_ge(s_tap, 4 * f + e + 1)
                                lag = 2 - tap
                                dve.scalar_tensor_tensor(y[:, b, lag:T], banks[:, b, e * T:(e + 1) * T - lag],
                                                         taps[:, j, 4 * e + tap:4 * e + tap + 1], y[:, b, lag:T],
                                                         ALU.mult, ALU.add).then_inc(s_tap, 1)
                    for kc in units:
                        ada_unit(third0, kc, i)
                    dve.wait_ge(s_silu, f0 + f + 1)
                    if conv:
                        dve.wait_ge(s_tap, 4 * f + 4)
                        dve.tensor_tensor(hid[:, b, :], sg[:, b, :], yv[:, b, :], ALU.mult).then_inc(freed[b], 1)
                    else:
                        dve.wait_ge(slot_used[up % RING], fills(up) + i)
                        dve.tensor_tensor(hid[:, b, :], sg[:, b, :], banks[:, b, T:2 * T], ALU.mult).then_inc(freed[b], 1)

                with dve.Fori(0, TURNS) as i:
                    for j in range(BODY):
                        chunk(i, j, [j])
                    modulation(third0, 3, ada_b, i)
                for j in range(FC - TURNS * BODY):
                    chunk(TURNS, j, ([0, 1], [2], [3, 4], [5], [6], [7])[j])
                residual_acc(third0 // 3 - 1)
                modulation(third0 + TURNS, 3, ada_b)
                norm_vector(2 * third0 // 3)
                norm_vector(2 * third0 // 3 + 1)

            dve.wait_ge(pos_in, 16)
            dve.wait_ge(cols_in, 16)
            chain = [0]

            def link(ins, s):
                chain[0] += 1
                ins.then_inc(s, 1)
                dve.wait_ge(s, chain[0])

            link(dve.tensor_copy(posf, posi), s_rope_dve)
            link(dve.tensor_scalar(ang, posf, col("inv_freq"), None, ALU.mult), s_rope_dve)
            link(dve.tensor_scalar(turns, ang, float(1 / (2 * np.pi)), MAGIC, ALU.mult, ALU.add), s_rope_dve)
            link(dve.tensor_scalar(turns, turns, MAGIC, None, ALU.subtract), s_rope_dve)
            for part in TWO_PI_PARTS:
                link(dve.scalar_tensor_tensor(ang, turns, -part, ang, ALU.mult, ALU.add), s_rope_dve)
            link(dve.tensor_scalar(ang, ang, PI_CLAMP, -PI_CLAMP, ALU.min, ALU.max), s_rope_dve)
            link(dve.memset(half_pi[:, :], float(np.pi / 2)), s_rope_dve)
            link(dve.tensor_scalar(negsink[:, :], col("rows", 8, 16), -1.0, None, ALU.mult), s_rope_dve)
            dve.wait_ge(s_cact, 1)
            for kc in range(KC):
                for half in range(2):
                    s = 2 * kc + half
                    ada_half(0, kc, half, ring[:, s, :], (slot_full[s], 16), (slot_used[s], 1))
                if kc == 3:
                    norm(0)
                    free_stat(0)
            modulation(0, 7, "ada_b")
            norm_vector(0)
            dve.wait_ge(s_xn, 8)
            for j in range(4):
                u = U["qkstat", j]
                dve.wait_ge(*u.done)
                if j:
                    dve.wait_ge(s_qk, 2 * j)
                dve.tensor_scalar(var[:, :], bank(u), 1.0 / HD, EPS, ALU.mult, ALU.add).then_inc(freed[u.bank], 1)
                dve.wait_ge(*taken(u))
                dve.reciprocal(var[:, :], var[:, :]).then_inc(s_qkvar, 1)
                dve.wait_ge(s_qkstd, j + 1)
                for e in range(2):
                    c = 2 * j + e
                    tile = (qT, kT)[c // 4][:, c % 4, :]
                    dve.wait_ge(*taken(U[("q", "k")[c // 4], c % 4]))
                    dve.scalar_tensor_tensor(tile, tile, col(("q_norm_g", "k_norm_g")[c // 4]), var[:, e * T:(e + 1) * T],
                                             ALU.mult, ALU.mult).then_inc(s_qk, 1)
            dve.wait_ge(bias_in, 32)
            between = {i: [lambda v=v: ada_unit(1 + v // 8, v % 8) for v in (2 * i, 2 * i + 1)] for i in range(8)}

            def first_half_gate():
                modulation(1, 7, "ada_b")
                dve.wait_ge(s_mod, 2)
                dve.tensor_scalar(ghalf[:, :], mod[:, 1, 0:8], 0.5, None, ALU.mult).then_inc(s_gate, 1)

            attend(first_heads, between)
            first_half_gate()
            for c in range(8):
                u = U["br", c]
                dve.wait_ge(*u.done)
                if c == 0:
                    dve.wait_ge(*taken(U["gp", 7]))
                    dve.wait_ge(*taken(U["gp", 6]))
                if c >= 2:
                    dve.wait_ge(s_merged, 2 * c - 2)
                dve.scalar_tensor_tensor(brt[:, c % 2, 0, :], ga[:, c, :], 1.0, bank(u, 0, T), ALU.add, ALU.mult).then_inc(s_merged, 1)
                dve.scalar_tensor_tensor(brt[:, c % 2, 1, :], gp[:, c, :], 1.0, bank(u, T, 2 * T), ALU.add, ALU.mult)\
                   .then_inc(freed[u.bank], 1)
                dve.wait_ge(s_merged, 2 * c + 1)
                dve.wait_ge(*taken(u))
                dve.tensor_tensor(merged[:, c, :], brt[:, c % 2, 0, :], brt[:, c % 2, 1, :], ALU.add).then_inc(s_merged, 1)
            modulation(2, 7, "ada_b")
            norm_vector(1)
            dve.wait_ge(s_gate, 1)
            residual_units("wo", ghalf)
            norm(1)
            free_stat(1)
            ffn("ffn1", True, 3, "e_ada_b")
            norm(2)
            free_stat(2)
            u = U["fgl"]
            dve.wait_ge(*u.done)
            dve.tensor_tensor(lf[:, 0, 0, :], bank(u, 0, 8), col("rows", 0, 8), ALU.add).then_inc(s_forget, 1)
            dve.tensor_tensor(lf[:, 0, 1, :], bank(u, 8, 16), col("rows", 0, 8), ALU.add).then_inc(freed[u.bank], 1)
            dve.wait_ge(s_forget, 4)
            dve.tensor_scalar(lf[:, 2], lf[:, 0], 0.0, None, ALU.min).then_inc(s_forget, 1)
            dve.wait_ge(s_forget, 5)
            dve.tensor_tensor(lf[:, 3], lf[:, 2], lf[:, 1], ALU.subtract).then_inc(s_forget, 1)
            u = U["cum"]
            dve.wait_ge(*u.done)
            dve.tensor_scalar(cum8[:, 0, :], bank(u, 0, T, 8), 1 / SCALE, None, ALU.mult).then_inc(s_cum8, 1)
            dve.tensor_scalar(cum8[:, 1, :], bank(u, 0, T, 8), -1 / SCALE, None, ALU.mult).then_inc(freed[u.bank], 1)
            between = {c + 1: [lambda c=c: rope(c, sqT[:, c, :], ("sq", c))] for c in range(4)}
            between[5] = [lambda: rope(4, skT, ("sk", 0))]
            attend(even_heads, between)
            residual_units("eo", mod[:, 4, 0:8])
            norm(3)
            free_stat(3)
            ffn("ffn2", False, 6, "o_ada_b")
            norm(4)
            free_stat(4)
            rope(5, ikT, ("ik", 0))
            for c in range(4):
                rope(6 + c, iqT[:, c, :], ("iq", c))
            for m in range(8):
                dve.wait_ge(s_relu, m + 1)
                if m == 0:
                    dve.wait_ge(*taken(U["iw"]))
                for j, (lo, hi) in enumerate(((0, HALF), (HALF, TRI))):
                    w = iws[:, j, m:m + 1]
                    if m == 0:
                        dve.tensor_scalar(score[:, lo:hi], relu[:, 0, lo:hi], w, None, ALU.mult).then_inc(s_isum, 1)
                    else:
                        dve.wait_ge(s_isum, 2 * m - 1 + j)
                        dve.scalar_tensor_tensor(score[:, lo:hi], relu[:, m % 2, lo:hi], w, score[:, lo:hi],
                                                 ALU.mult, ALU.add).then_inc(s_isum, 1)
            dve.wait_ge(s_isum, 16)
            dve.tensor_tensor(work, score, causal, ALU.add).then_inc(s_isum, 1)
            dve.wait_ge(s_isum, 17)

            def top_rounds(r0):
                for r in (r0, r0 + 1):
                    for j, (lo, hi) in enumerate(((0, HALF), (HALF, TRI))):
                        if r:
                            dve.wait_ge(s_topk, 4 * r - 1 + j)
                        dve.max(top8[:, j, :], work[:, lo:hi]).then_inc(s_topk, 1)
                    for j, (lo, hi) in enumerate(((0, HALF), (HALF, TRI))):
                        dve.wait_ge(s_topk, 4 * r + 1 + j)
                        dve.match_replace(work[:, lo:hi], top8[:, j, :], work[:, lo:hi], TAKEN).then_inc(s_topk, 1)

            rope(10, dkT[:, 0, :], ("dk", 0))
            top_rounds(0)
            rope(11, dkT[:, 1, :], ("dk", 1))
            top_rounds(2)
            rope(12, dqT[:, 0, :], ("dq", 0))
            top_rounds(4)
            rope(13, dqT[:, 1, :], ("dq", 1))
            top_rounds(6)
            rope(14, dqT[:, 2, :], ("dq", 2))
            dve.wait_ge(s_topk, 32)
            dve.tensor_scalar(dmask, work, TAKEN / 2, -BIG, ALU.is_gt, ALU.mult).then_inc(s_dmask, 1)
            dve.wait_ge(s_dmask, 1)
            dve.tensor_tensor(dmask, dmask, causal, ALU.add).then_inc(s_dmask, 1)
            dve.wait_ge(s_dmask, 2)
            attend(odd_heads, {2 * (c - 3): [lambda c=c: rope(12 + c, dqT[:, c, :], ("dq", c))] for c in range(3, 8)})
            residual_units("oo", mod[:, 7, 0:8])
            norm(5)
            free_stat(5)

            def two(a, n):
                return rt[:, a:a + 2 * n].rearrange("p (a e) -> p a e", a=2)

            picked, lwork, v8, rep8, marked = two(0, 8), two(16, 16), two(48, 8), two(64, 8), two(80, 16)
            lg, den, rden, comb, rank = two(112, 8), rt[:, 128:130], rt[:, 130:132], two(132, 8), two(148, 8)
            count, over, pre, pre2, slotno = rt[:, 164:172], rt[:, 172:188], rt[:, 188:204], rt[:, 204:220], rt[:, 220:236]
            match = rt[:, 236:236 + 16 * EXTRA].rearrange("p (q c) -> p q c", q=EXTRA)
            ranks2, comb2 = two(316, 16), two(348, 16)
            prod = rt[:, 380:380 + 16 * EXTRA].rearrange("p (q c) -> p q c", q=EXTRA)
            chain[0] = 0
            dve.wait_ge(s_o, 20)
            dve.memset(yT, 0.0).then_inc(s_yT_dve, 1)
            dve.memset(pickT, 0.0).then_inc(s_init, 1)
            dve.memset(lwork[:, :, 8:16], TAKEN).then_inc(s_route, 1)
            dve.memset(rep8[:, :, 2:8], TAKEN).then_inc(s_route, 1)
            u = U["router"]
            dve.wait_ge(*u.done)
            dve.tensor_tensor(lwork[:, 0, 0:8], bank(u, 0, 8), col("rows", 16, 24), ALU.add).then_inc(s_route, 1)
            dve.tensor_tensor(lwork[:, 1, 0:8], bank(u, 8, 16), col("rows", 16, 24), ALU.add).then_inc(freed[u.bank], 1)
            dve.wait_ge(s_route, 3)
            dve.wait_ge(*taken(u))
            dve.max(v8[:, 0, :], lwork[:, 0, 0:8]).then_inc(s_route, 1)
            dve.max(v8[:, 1, :], lwork[:, 1, 0:8]).then_inc(s_route, 1)
            chain[0] = 5
            dve.wait_ge(s_route, 5)
            link(dve.tensor_copy(rep8[:, :, 0:2], v8[:, :, 0:2]), s_route)
            for tile in range(2):
                link(dve.match_replace(marked[:, tile, :], rep8[:, tile, :], lwork[:, tile, :], -TAKEN), s_route)
            link(dve.tensor_scalar(picked, marked[:, :, 0:8], -TAKEN / 2, None, ALU.is_gt), s_route)
            assert chain[0] == 9
            for tile in range(2):
                link(dve.tensor_scalar(lg[:, tile, :], lwork[:, tile, 0:8], v8[:, tile, 0:1], None, ALU.subtract), s_route)
            dve.wait_ge(s_gexp, 1)
            link(dve.tensor_tensor(comb, lg, picked, ALU.mult), s_route)
            link(dve.tensor_reduce(den, comb, AX, ALU.add), s_route)
            link(dve.reciprocal(rden, den), s_route)
            for tile in range(2):
                link(dve.tensor_scalar(comb[:, tile, :], comb[:, tile, :], rden[:, tile:tile + 1], None, ALU.mult), s_route)
            u = U["ranks"]
            dve.wait_ge(*u.done)
            link(dve.tensor_tensor(rank, bank(u, 0, 16).rearrange("p (a e) -> p a e", a=2), picked, ALU.mult), s_route)
            dve.tensor_copy(count, bank(u, 16, 24)).then_inc(freed[u.bank], 1)
            dve.wait_ge(*taken(u))
            link(dve.memset(tab, 0.0), s_route)
            for tile in range(2):
                link(dve.tensor_copy(tab[:, 0:EXPERTS, tile], rank[:, tile, :]), s_route)
                link(dve.tensor_copy(tab[:, 0:EXPERTS, 2 + tile], comb[:, tile, :]), s_route)
            link(dve.tensor_copy(cur, tab[:, 0, :]), s_route)
            iota = mat("iota")
            for tile in range(2):
                dve.tensor_scalar(pick[:, tile, :], iota, cur[:, tile:tile + 1], None, ALU.is_equal).then_inc(s_pick, 1)
            link(dve.tensor_scalar(over[:, 0:8], count, float(CAP), None, ALU.is_gt), s_route)
            link(dve.tensor_scalar(over[:, 8:16], count, float(2 * CAP), None, ALU.is_gt), s_route)
            link(dve.tensor_copy(pre, over), s_route)
            a, b = pre, pre2
            for shift in (1, 2, 4, 8):
                link(dve.tensor_copy(b[:, 0:shift], a[:, 0:shift]), s_route)
                link(dve.tensor_tensor(b[:, shift:16], a[:, shift:16], a[:, 0:16 - shift], ALU.add), s_route)
                a, b = b, a
            link(dve.tensor_tensor(slotno, a, over, ALU.mult), s_route)
            for q in range(EXTRA):
                link(dve.tensor_scalar(match[:, q, :], slotno, float(q + 1), None, ALU.is_equal), s_route)
            cand_expert, cand_block = mat("small", 0, 16), mat("small", 16, 32)
            for tile in range(2):
                for half in range(2):
                    link(dve.scalar_tensor_tensor(ranks2[:, tile, 8 * half:8 * half + 8], cand_block[:, 8 * half:8 * half + 8],
                                                  -float(CAP), rank[:, tile, :], ALU.mult, ALU.add), s_route)
                    link(dve.tensor_copy(comb2[:, tile, 8 * half:8 * half + 8], comb[:, tile, :]), s_route)
            extra = slice(EXPERTS, EXPERTS + EXTRA)
            for k, source in enumerate((ranks2[:, 0, :], ranks2[:, 1, :], comb2[:, 0, :], comb2[:, 1, :], cand_expert)):
                for q in range(EXTRA):
                    link(dve.tensor_tensor(prod[:, q, :], match[:, q, :], source, ALU.mult), s_route)
                if k < 4:
                    link(dve.tensor_reduce(tab[:, extra, k], prod, AX, ALU.add), s_route)
            link(dve.tensor_reduce(rt[:, 460:460 + EXTRA], prod, AX, ALU.add), s_route)
            link(dve.tensor_copy(ints[:, 0:EXPERTS], cand_expert[:, 0:EXPERTS]), s_route)
            link(dve.tensor_copy(ints[:, extra], rt[:, 460:460 + EXTRA]), s_route)
            link(dve.tensor_scalar(ints[:, NTAB:NTAB + 1], a[:, 15:16], float(EXPERTS), None, ALU.add), s_route)
            dve.engine_nop().then_inc(s_routed, 1)
            m0 = U["moe"]
            before = [len(range(s, m0.pos, RING)) if s < RING else 0 for s in range(MSLOTS)]
            passes = dve.value_load(ints[0:1, NTAB:NTAB + 1], min_val=EXPERTS, max_val=EXPERTS + EXTRA)

            def token_major(p, b, half, aux):
                dve.wait_ge(aux_done, m0.done + 5 * p + aux)
                dve.tensor_copy(y_tok[:, half * 512:(half + 1) * 512], banks[0:CAP, b, :]).then_inc(freed[b], 1)

            with dve.Fori(0, passes) as p:
                for tile in range(2):
                    dve.tensor_scalar(cpick[:, tile, :], iota, cur[:, tile:tile + 1], cur[:, 2 + tile:3 + tile],
                                      ALU.is_equal, ALU.mult).then_inc(s_cpick, 1)
                for f in range(EF):
                    r = (0, 3)[f] if f < 2 else f + 3
                    dve.wait_ge(s_silu, 2 * FC + EF * p + f + 1)
                    dve.wait_ge(slot_used[3 * f + 1], before[3 * f + 1] + p + 1)
                    dve.tensor_tensor(ehid[:, f % 2, :], esg[:, f % 2, :], banks[:, r % 2, T:T + CAP], ALU.mult).then_inc(freed[r % 2], 1)
                    if f == 0:
                        token_major(p, 0, 1, 2)
                    if f == 1:
                        dve.wait_ge(aux_done, m0.done + 5 * p + 3)
                        dve.tensor_copy(pickT, banks[0:CAP, 0, 0:T]).then_inc(freed[0], 1)
                    if f == 3:
                        dve.wait_ge(s_cpick, 2 * p + 2)
                        dve.tensor_copy(cur, tab[:, bass.ds(p + 1, 1), :].rearrange("p a n -> p (a n)")).then_inc(s_cur, 1)
                        dve.wait_ge(s_cur, p + 1)
                        for tile in range(2):
                            dve.tensor_scalar(pick[:, tile, :], iota, cur[:, tile:tile + 1], None, ALU.is_equal).then_inc(s_pick, 1)
                dve.wait_ge(aux_done, m0.done + 5 * p + 4)
                dve.tensor_copy(hg[:, 0:4, :].rearrange("p a n -> p (a n)"), banks[:, 0, 0:4 * CAP]).then_inc(freed[0], 1)
                dve.wait_ge(slot_used[MSLOTS - 1], before[MSLOTS - 1] + p + 1)
                dve.tensor_copy(yT[:, 4:8, :].rearrange("p a n -> p (a n)"), banks[:, 3, 0:4 * CAP]).then_inc(s_yT_dve, 1)
            token_major(passes, 1, 1, 2)
            residual_acc(2)
            norm(6, banks[:, 0, 0:T], (aux_done, m0.done + 5 * passes + 3))


def _bucket(dist):
    n = np.maximum(dist, 0)
    nf = np.maximum(n, 1).astype(np.float32)
    large = 16 + (np.log(nf / np.float32(16)) / np.float32(np.log(8.0)) * np.float32(16)).astype(np.int32)
    return np.where(n < 16, n, np.minimum(large, 31))


def _constants():
    mats = np.zeros((P, NMATS), np.float32)

    def put(name, value):
        at, n = MATS[name]
        mats[:value.shape[0], at:at + n] = value

    p, t = np.arange(P)[:, None], np.arange(T)[None, :]
    put("ident", np.eye(P))
    put("heads", (p // HD == np.arange(P)[None, :] // HD) * 1.0)
    k, m = p, np.arange(P)[None, :]
    put("rotate", (k == m - 32) * (m % HD >= 32) * 1.0 - (k == m + 32) * (m % HD < 32) * 1.0)
    dist = np.concatenate([p - np.arange(HALF)[None, :], HALF + p - t], 1)
    put("causal", np.where(dist >= 0, 0.0, -BIG))
    put("band", np.where((dist >= 0) & (dist < 128), 0.0, -BIG))
    put("upto", np.concatenate([p <= t, p + HALF <= t], 1) * 1.0)
    put("iota", np.broadcast_to(np.arange(1, CAP + 1), (P, CAP)))
    small = np.zeros((P, 64))
    small[:, 0:16] = np.arange(16) % 8
    small[:, 16:32] = 1 + np.arange(16) // 8
    put("small", small)
    onehot = np.zeros((33, 512), np.float32)
    d = 255 - np.arange(512)
    onehot[_bucket(d), np.arange(512)] = d >= 0
    onehot[32] = np.where(d >= 0, 0.0, -BIG)
    pool = np.zeros((T, 4, T), np.float32)
    src, dst = np.arange(T)[:, None], np.arange(T)[None, :]
    for g, w in enumerate((2, 4, 8, 16)):
        inside = (src <= dst) & (src > dst - w)
        pool[:, g, :] = inside / np.minimum(dst + 1, w).astype(np.float32) - (src == dst)
    pool = np.ascontiguousarray(pool.reshape(2, P, 4, T).transpose(1, 0, 2, 3))
    sel = np.zeros((8, 8, T), np.float32)
    sel[np.arange(8), np.arange(8)] = 1.0
    inv_freq = (np.float32(10000.0) ** (-np.arange(32, dtype=np.float32) / np.float32(32))).astype(np.float32)
    return mats, onehot, pool, sel, inv_freq


def _tiles(w, columns=None):
    w = w if columns is None else w[:, columns]
    return w.reshape(KC, P, -1, P).transpose(2, 1, 0, 3).reshape(-1, P, SLOT)


def _rows(w, slots, width):
    return w.reshape(slots, KC // slots, P, width).transpose(0, 2, 1, 3).reshape(slots, P, SLOT)


def _ffn(gate, up, down):
    return np.stack([_tiles(gate), _tiles(up), down.reshape(-1, P, SLOT)], 1).reshape(-1, P, SLOT)


def _columns(v):
    return v.reshape(-1, P).T


def kernel(**inputs):
    import concourse.bacc as bacc
    from concourse.bass_utils import run_bass_kernel_spmd

    a = {name: np.asarray(value) for name, value in inputs.items()}
    f = lambda name: a[name][0]
    mats, onehot, pool, sel, inv_freq = _constants()
    swa = np.concatenate([np.arange(64) + 64 * (j + 4 * half) for j in range(4) for half in range(2)])
    dsa = np.concatenate([np.arange(64) + 64 * (8 * (j // 4) + j % 4 + 4 * half) for j in range(8) for half in range(2)])
    w_in, ew, ow = f("w_in"), f("e_w_in_2"), f("o_w_in_2")
    branch = np.concatenate([f("w_branch_attn").reshape(4, P, 8, P), f("w_branch_pool").reshape(4, P, 8, P)], 0)
    ada = f("ada_w")
    half = 2816
    parts = [
        ada[:, 0:2048].reshape(KC, P, 2, SLOT).transpose(0, 2, 1, 3).reshape(16, P, SLOT),
        _tiles(w_in[:, 0:1024]), _rows(w_in[:, 1024:1536], 4, 512), _rows(w_in[:, 1536:2048], 4, 512),
        _tiles(w_in[:, 2048:4096]), branch.transpose(2, 1, 0, 3).reshape(8, P, SLOT), _tiles(f("w_out")),
        _ffn(f("w_up")[:, :half], f("w_up")[:, half:], f("w_down")),
        _tiles(ew[:, 0:1024]), _rows(ew[:, 1024:1536], 4, 512), _tiles(ew[:, 1544:2056], swa), _tiles(ew[:, 2056:2184]),
        _rows(ew[:, 2184:2312], 1, 128), _tiles(f("e_w_out_2")[np.concatenate([np.arange(512), 512 + swa])]),
        _ffn(f("e_ffn_gate_2"), f("e_ffn_up_2"), f("e_ffn_down_2")),
        _tiles(np.concatenate([ow[:, 2048:2112]] * 2, 1)), _tiles(ow[:, 1536:2048]), _tiles(ow[:, 1024:1280]),
        _rows(ow[:, 1280:1536], 2, 256), _tiles(ow[:, 0:1024], dsa), _tiles(f("o_w_out_2")[dsa]),
    ]
    stream = np.concatenate(parts)
    experts = np.concatenate([_ffn(f("o_exp_gate_2")[e], f("o_exp_up_2")[e], f("o_exp_down_2")[e]) for e in range(EXPERTS)])
    conv = np.stack([*f("conv_w"), f("conv_b")]).reshape(4, 2, FC, P).transpose(3, 2, 1, 0).reshape(P, 8 * FC)
    wide = lambda v: np.broadcast_to(v, (P, v.size))
    small = lambda w: w.reshape(KC, P, 8).transpose(1, 0, 2).reshape(P, 64)
    cols = np.concatenate([
        *[_columns(a[n]) for n in ("norm1_g", "norm2_g", "e_norm_mix_2", "e_norm_ffn_2", "o_norm_mix_2", "o_norm_ffn_2",
                                   "final_norm_2", "ada_b", "e_ada_b_2", "o_ada_b_2", "pool_scale")],
        np.tile(f("q_norm_g"), 2)[:, None], np.tile(f("k_norm_g"), 2)[:, None], conv, _columns(a["c"]), _columns(a["c_2"]),
        np.tile(inv_freq, 4)[:, None], wide(f("e_forget_b_2")), wide(f("e_sinks_2")), wide(f("o_router_b_2")),
        small(ew[:, 1536:1544]), small(ow[:, 2112:2120]), small(f("o_router_w_2"))], 1)
    relb = np.concatenate([a["rel_bias"], np.ones((1, 8), np.float32)])
    arrays = {
        "xT": a["x"][0].T.reshape(KC, P, T).transpose(1, 0, 2), "cols": cols, "mats": mats,
        "positions": np.broadcast_to(a["positions_2"].reshape(1, T), (P, T)), "onehot": onehot,
        "relb": np.broadcast_to(relb[:, :, None], (33, 8, P)), "sel": sel, "poolA": pool,
        "poolw": f("pool_w").transpose(1, 0, 2), "stream": stream, "ada1": ada, "ada2": f("e_ada_w_2"),
        "ada3": f("o_ada_w_2"), "experts": experts}
    arrays = {name: np.ascontiguousarray(v) for name, v in arrays.items()}
    nc = bacc.Bacc("TRN2", target_bir_lowering=False, num_devices=1)
    args = [nc.dram_tensor(name, v.shape, mybir.dt.from_np(v.dtype), kind="ExternalInput").ap() for name, v in arrays.items()]
    out = nc.dram_tensor("out_0_dram", (P, KC, T), F32, kind="ExternalOutput").ap()
    program(nc, *args, out)
    r = run_bass_kernel_spmd(nc, [arrays], core_ids=[0])
    y = r.results[0]["out_0_dram"]
    return np.ascontiguousarray(y.transpose(2, 1, 0).reshape(1, T, D))
```

```python
from contextlib import ExitStack

import numpy as np

import concourse.bass as bass
from concourse import mybir

F32 = mybir.dt.float32
BF16 = mybir.dt.bfloat16
I32 = mybir.dt.int32
ACT = mybir.ActivationFunctionType
ALU = mybir.AluOpType
AX = mybir.AxisListType.X

P = 128
D = 1024
T = 256
KC = D // P
HALF = T // 2
TRI = HALF + T
HD = 64
SLOT = 1024
RING = 24
FC = 2816 // P
BODY = RING // 3
TURNS = FC // BODY
EXPERTS = 8
EF = 1408 // P
MSLOTS = 3 * EF
CAP = 96
EXTRA = (2 * T) // (CAP + 1)
NTAB = EXPERTS + EXTRA + 1
USES = EF + 3
LAG = 2
BIG = 1.0e30
TAKEN = -3.0e38
EPS = 1e-6
SCALE = HD ** -0.5
MAGIC = 12582912.0
TWO_PI_PARTS = (6.28125, 0.0019350051879882812, 3.0198999e-07)
PI_CLAMP = 3.1415925

COLS = {}
for _name, _n in (("norm1_g", 8), ("norm2_g", 8), ("e_norm_mix", 8), ("e_norm_ffn", 8), ("o_norm_mix", 8),
                  ("o_norm_ffn", 8), ("final_norm", 8), ("ada_b", 48), ("e_ada_b", 48), ("o_ada_b", 48),
                  ("pool_scale", 4), ("q_norm_g", 1), ("k_norm_g", 1), ("conv", 8 * FC),
                  ("inv_freq", 1), ("rows", 24), ("fgl", 64), ("iw", 64), ("router", 64)):
    COLS[_name] = (sum(n for _, n in COLS.values()), _n)
NCOLS = sum(n for _, n in COLS.values())
NORM_GAINS = ("norm1_g", "norm2_g", "e_norm_mix", "e_norm_ffn", "o_norm_mix", "o_norm_ffn", "final_norm")

MATS = {}
for _name, _n in (("ident", 128), ("heads", 128), ("rotate", 128), ("causal", TRI), ("band", TRI),
                  ("upto", T), ("iota", CAP), ("small", 64)):
    MATS[_name] = (sum(n for _, n in MATS.values()), _n)
NMATS = sum(n for _, n in MATS.values())


class Unit:

    def __init__(self, bank, nth, pos, done):
        self.bank, self.nth, self.pos, self.done = bank, nth, pos, done


def plan_units(slot_used, aux_done):
    units = {}
    at = {"bank": 0, "nth": [0, 0], "pos": 16, "aux": 0}

    def add(name, slots=0, release=True):
        pos, bank = at["pos"], at["bank"]
        if slots and release:
            last = pos + slots - 1
            done = (slot_used[last % RING], last // RING + 1)
            at["pos"] += slots
        else:
            at["aux"] += 1
            done = (aux_done, at["aux"])
        units[name] = Unit(bank, at["nth"][bank], pos, done)
        at["nth"][bank] += 1
        at["bank"] = 1 - bank

    def loop(name):
        units[name] = Unit(0, tuple(at["nth"]), at["pos"], at["aux"])
        at["nth"] = [n + FC // 2 for n in at["nth"]]
        at["bank"] = 0
        at["pos"] += 3 * FC

    def add_all(name, n, slots=1):
        for c in range(n):
            add((name, c), slots)

    add(("stat", 0))
    add_all("t5", 8, 0)
    add_all("q", 4)
    add(("qkstat", 0))
    add(("k", 0), 1)
    add(("k", 1), 1)
    add(("qkstat", 1))
    add(("k", 2), 1)
    add(("k", 3), 1)
    add(("qkstat", 2))
    add(("v", 0), 4, release=False)
    add(("v", 1), 4)
    add(("qkstat", 3))
    add(("p", 0), 4, release=False)
    add(("p", 1), 4)
    add_all("pool", 2, 0)
    add_all("poolw", 2, 0)
    add_all("ga", 8)
    add_all("gp", 8)
    add_all("br", 8)
    add_all("wo", 8)
    loop("ffn1")
    add(("stat", 2))
    add("fgl")
    add(("fq", 0), 1)
    add("fglT")
    for c in range(1, 4):
        add(("fq", c), 1)
    add_all("fk", 4)
    add("cum")
    add(("fv", 0), 4, release=False)
    add(("fv", 1), 4)
    add(("sq", 0), 1)
    for c in range(1, 4):
        add(("sq", c), 1)
        add(("rot", c - 1))
    add(("sk", 0), 1)
    add(("rot", 3))
    add("sv", 1)
    add(("rot", 4))
    add_all("eo", 8)
    loop("ffn2")
    add(("stat", 4))
    add("iw")
    add(("ik", 0), 1)
    add("iwT")
    for c in range(4):
        add(("iq", c), 1)
        add(("rot", 5 + c))
    add(("dk", 0), 1)
    add(("rot", 9))
    add(("dk", 1), 1)
    add(("rot", 10))
    add("dv", 2)
    add(("rot", 11))
    add(("dq", 0), 1)
    for c in range(1, 8):
        add(("dq", c), 1)
        add(("rot", 11 + c))
    add(("rot", 19))
    add_all("oo", 8)
    add("router")
    add(("htok", 0))
    add(("htok", 1))
    add("routerT")
    add(("htok", 2))
    add(("htok", 3))
    add("ranks")
    add_all("gather", 2, 0)
    units["moe"] = Unit(0, tuple(at["nth"]), at["pos"], at["aux"])
    return units


def norm_scale_source(r):
    layer, ffn = divmod(r, 2)
    return ((3 * layer + 1, 8), (3 * layer + 2, 0)) if ffn else ((3 * layer, 0), (3 * layer, 8))


def program(nc, xT, cols_d, mats_d, pos_d, onehot_d, relb_d, sel_d, poolA_d, poolw_d, stream, cond_d, ada,
            experts, out):
    ctx = ExitStack()
    with ctx:
        def sb(name, shape, dt=F32):
            return ctx.enter_context(nc.sbuf_tensor(name, shape, dt))

        def sem(name):
            return ctx.enter_context(nc.semaphore(name))

        ring = sb("ring", [P, RING, SLOT])
        x = sb("x", [P, KC, T])
        h = sb("h", [P, KC, T])
        side = sb("side", [P, 6, SLOT])
        arena = sb("arena", [P, 12288])
        cols = sb("vectors", [P, NCOLS])
        mats = sb("constants", [P, NMATS])
        ones = sb("ones", [P, P])
        zeros = sb("zeros", [1, P], BF16)
        cos = sb("cos", [P, T])
        sin = sb("sin", [P, T])
        mod = sb("mod", [P, 9, 16])
        avec = sb("avec", [P, 7, 8])
        ghalf = sb("ghalf", [P, 8])
        msum = sb("msum", [P, 16])
        eps = sb("eps", [P, 1])
        warm = sb("warm", [P, 8])
        negsink = sb("negsink", [P, 8])
        half_pi = sb("half_pi", [P, 1])
        var = sb("var", [P, 512])
        rstd = var[:, T:2 * T]
        logit = sb("logit", [P, LAG + 1, TRI])
        probT = sb("probT", [P, 2, TRI])
        few = probT[0:8, 0, 0:T]
        stats = sb("stats", [P, LAG + 1, 8])
        banks = ctx.enter_context(nc.psum_tensor("banks", [P, 8, 512], F32))

        def mat(name, a=0, b=None):
            at, n = MATS[name]
            return mats[:, at + a:at + (n if b is None else b)]

        def col(name, a=0, b=None):
            at, n = COLS[name]
            return cols[:, at + a:at + (n if b is None else b)]

        def region(kib, shape, parts=P):
            n = int(np.prod(shape))
            flat = arena[0:parts, int(kib * 256):int(kib * 256) + n]
            if len(shape) == 1:
                return flat
            names = "abc"[:len(shape)]
            return flat.rearrange(f"p ({' '.join(names)}) -> p {' '.join(names)}",
                                  **{names[j]: shape[j] for j in range(len(shape) - 1)})

        ada_slot = side[:, 0:4, :].rearrange("p (s a) n -> p s (a n)", s=2)
        cond = side[:, 4:6, :]
        ident = mat("ident")
        finite = mats[0:1, 0:T].bitcast(BF16)
        causal, band = mat("causal"), mat("band")
        upto = mat("upto")

        def moe_slot(m):
            return ring[:, m, :] if m < RING else (
                side[:, m - RING, :] if m < RING + 6 else arena[:, (m - RING - 6) * SLOT:(m - RING - 5) * SLOT])

        qT, kT = region(0, [4, T]), region(4, [4, T])
        onehot, relb = region(0, [512], 33), region(2, [8, P], 33)
        v_tok, p_tok = region(8, [2, 512]), region(12, [2, 512])
        pool2 = region(12, [4, T])
        ga, gp = region(16, [8, T]), region(24, [8, T])
        t5rows = region(16, [8, 512])
        poolw, poolT = region(16, [4, P]), region(18, [4, T])
        poolA = region(24, [2, 4, T])
        bias = region(32, [8, TRI])
        oT1 = region(44, [4, T])
        qksq = region(44, [4, T])
        merged = region(0, [8, T])
        brt = region(32, [2, 2, T])
        ang, turns, posf = region(32, [T]), region(33, [T]), region(34, [T])
        posi = region(35, [T]).bitcast(I32)
        yg, yv, sg, hid = region(12, [2, T]), region(14, [2, T]), region(16, [2, T]), region(18, [2, T])
        taps = region(20, [BODY, 8])
        fqT, fkT, fv = region(0, [4, T]), region(4, [4, T]), region(8, [2, 512])
        sqT, skT, sv = region(12, [4, T]), region(16, [T]), region(17, [2, P])
        sel = region(18, [8, T], 72)
        lf = region(26, [3, 2, 8])
        lf72 = region(26.25, [2, 72])
        cum = region(27, [T], 72)
        ropet = region(29, [2, T])
        oT2 = region(32, [8, T])
        dqT, dkT, dv = region(0, [8, T]), region(8, [2, T]), region(10, [2, T])
        iqT, ikT = region(12, [4, T]), region(16, [T])
        score, work, dmask = region(17, [TRI]), region(18.5, [TRI]), region(20, [TRI])
        relu = region(21.5, [2, TRI])
        iws, top8 = region(24.5, [2, 8]), region(25, [2, 8])
        htok = region(12, [2, D])
        hg = region(20, [KC, CAP])
        ehid, esg = region(23, [2, CAP]), region(24, [2, CAP])
        y_tok = region(28, [D], CAP)
        pickT = region(32, [T], CAP)
        pick, cpick = region(33, [2, CAP]), region(34, [2, CAP])
        rt = region(35, [1024])
        tab = region(39, [NTAB, 4])
        cur = region(39.5, [4])
        ints = region(40, [NTAB + 1]).bitcast(I32)

        slot_full = [sem(f"slot_full{s}") for s in range(MSLOTS)]
        slot_used = [sem(f"slot_used{s}") for s in range(MSLOTS)]
        ada_full = [sem(f"ada_full{s}") for s in range(2)]
        cond_in = [sem(f"cond_in{n}") for n in range(2)]
        x_in, cols_in, mats_in, pos_in, onehot_in = (sem(n) for n in ("x_in", "cols_in", "mats_in", "pos_in", "onehot_in"))
        t5_stored, bias_in, pool_in, sel_in, out_stored = (sem(n) for n in ("t5_stored", "bias_in", "pool_in", "sel_in", "out_stored"))
        consts_set = sem("consts_set")
        aux_done = sem("aux_done")
        freed = [sem("freed0"), sem("freed1")]
        s_cact, s_rope_dve, s_rope_act = sem("s_cact"), sem("s_rope_dve"), sem("s_rope_act")
        s_ada, s_mod, s_avec = sem("s_ada"), sem("s_mod"), sem("s_avec")
        s_sq, s_sum, s_root, s_rstd, s_xn, s_h = (sem(n) for n in ("s_sq", "s_sum", "s_root", "s_rstd", "s_xn", "s_h"))
        s_qksq, s_qkrstd, s_qk = sem("s_qksq"), sem("s_qkrstd"), sem("s_qk")
        s_score, s_logit, s_exp, s_rsum, s_prob = (sem(n) for n in ("s_score", "s_logit", "s_exp", "s_rsum", "s_prob"))
        s_tr, s_pt, s_pv, s_o = (sem(n) for n in ("s_tr", "s_pt", "s_pv", "s_o"))
        s_gate, s_merged = sem("s_gate"), sem("s_merged")
        s_taps_in, s_conv, s_tap, s_silu, s_acc, s_x = (sem(n) for n in ("s_taps_in", "s_conv", "s_tap", "s_silu", "s_acc", "s_x"))
        s_forget, s_cum = sem("s_forget"), sem("s_cum")
        s_rot, s_rope = sem("s_rot"), sem("s_rope")
        s_iscore, s_relu, s_isum, s_topk, s_dmask = (sem(n) for n in ("s_iscore", "s_relu", "s_isum", "s_topk", "s_dmask"))
        s_route, s_routed, s_gexp, s_pick, s_cpick, s_cur = (sem(n) for n in ("s_route", "s_routed", "s_gexp", "s_pick", "s_cpick", "s_cur"))
        s_y_act, s_y_dve, s_passes = (sem(n) for n in ("s_y_act", "s_y_dve", "s_passes"))
        s_final, s_pool = sem("s_final"), sem("s_pool")

        U = plan_units(slot_used, aux_done)
        scratch = nc.dram_tensor("bias_rows", (8 * P * 512,), F32, kind="Internal").ap()

        def taken(u):
            return freed[u.bank], u.nth + 1

        def bank(u, a=0, b=512, parts=P):
            return banks[0:parts, u.bank, a:b]

        def use_of(f):
            return f if f < 2 else f + 1

        def fills(pos):
            return pos // RING + 1

        def norm_bank(r):
            if ("stat", r) in U:
                u = U["stat", r]
                return u.bank, u.done, taken(u)
            return (0 if r == 6 else 7), (s_sum, (r + 2) // 2), (s_root, (r + 2) // 2)

        class Heads:
            pass

        def heads_of(n0, count, kind):
            found = []
            for i in range(count):
                a = Heads()
                a.n = n0 + i
                a.chunk, a.half = i // 2, i % 2
                a.kind = kind
                rows = slice(64 * a.half, 64 * a.half + 64)
                if kind == "moba":
                    a.q, a.k, a.v = qT[rows, a.chunk], kT[rows, a.chunk], v_tok
                    a.vcol, a.bias, a.out = 64 * i, bias[:, i, :], oT1[:, a.chunk]
                elif kind == "fox":
                    a.q, a.k, a.v = fqT[rows, a.chunk], fkT[rows, a.chunk], fv
                    a.vcol, a.bias, a.out = 64 * i, causal, oT2[:, a.chunk]
                elif kind == "swa":
                    a.q, a.k, a.v = sqT[rows, a.chunk], skT[rows, :], sv
                    a.vcol, a.bias, a.out = 64 * a.half, band, oT2[:, 4 + a.chunk]
                    a.sink = a.chunk + 4 * a.half
                else:
                    a.q, a.k, a.v = dqT[rows, a.chunk], dkT[rows, a.chunk // 4], dv
                    a.vcol, a.bias, a.out = 128 * (a.chunk // 4) + 64 * a.half, dmask, dqT[:, a.chunk]
                a.i = i
                found.append(a)
            return found

        first_heads = heads_of(0, 8, "moba")
        even_heads = heads_of(8, 8, "fox") + heads_of(16, 8, "swa")
        odd_heads = heads_of(24, 16, "dsa")

        def exp_count(n):
            return 2 * n + 2 + min(max(n - 15, 0), 8)

        def rsum_count(n):
            return n + 1 + min(max(n - 15, 0), 8)

        def x_ready(m, c):
            if m % 2:
                return s_x, 8 * (m // 2) + c + 1
            return taken(U[("wo", "eo", "oo")[m // 2], c])

        block = ctx.enter_context(nc.Block())

        @block.sync
        def _(sp):
            sp.dma_start(cols[:, :], cols_d).then_inc(cols_in, 16)
            sp.dma_start(posi, pos_d).then_inc(pos_in, 16)
            sp.dma_start(cond[:, 0, :], cond_d[0:1, :].broadcast_to([P, D])).then_inc(cond_in[0], 16)
            sp.dma_start(x[:, :, :], xT).then_inc(x_in, 16)
            for s in range(RING):
                sp.dma_start(ring[:, s, :], stream[s]).then_inc(slot_full[s], 16)
                if s == 17:
                    sp.dma_start(mats[:, :], mats_d).then_inc(mats_in, 16)
            total = U["moe"].pos
            whole = total // RING
            with sp.Fori(1, whole) as t:
                for s in range(RING):
                    sp.wait_ge(slot_used[s], t)
                    sp.dma_start(ring[:, s, :],
                                 stream[bass.ds(t * RING + s, 1)].rearrange("a p n -> p (a n)")).then_inc(slot_full[s], 16)
            for pos in range(whole * RING, total):
                s = pos % RING
                sp.wait_ge(slot_used[s], whole)
                sp.dma_start(ring[:, s, :], stream[pos]).then_inc(slot_full[s], 16)
            before = [len(range(s, total, RING)) if s < RING else 0 for s in range(MSLOTS)]
            for m in range(MSLOTS):
                if m < RING:
                    sp.wait_ge(slot_used[m], before[m])
                elif m == RING:
                    sp.wait_ge(s_mod, 9)
                elif m == RING + 6:
                    sp.wait_ge(s_o, 20)
                    sp.wait_ge(U["oo", 7].done[0], U["oo", 7].done[1])
                sp.dma_start(moe_slot(m), experts[m]).then_inc(slot_full[m], 16)
            sp.wait_ge(s_routed, 1)
            passes = sp.value_load(ints[0:1, NTAB:NTAB + 1], min_val=EXPERTS, max_val=EXPERTS + EXTRA)
            with sp.Fori(1, passes) as p:
                expert = sp.value_load(ints[0:1, bass.ds(p, 1)], min_val=0, max_val=EXPERTS - 1)
                for m in range(MSLOTS):
                    sp.wait_ge(slot_used[m], before[m] + p)
                    sp.dma_start(moe_slot(m),
                                 experts[bass.ds(expert * MSLOTS + m, 1)].rearrange("a p n -> p (a n)")).then_inc(slot_full[m], 16)
            for c in range(0, KC, 2):
                sp.wait_ge(s_final, c + 2)
                sp.dma_start(out[:, c:c + 2, :], h[:, c:c + 2, :]).then_inc(out_stored, 16)
            sp.wait_ge(out_stored, 64)

        @block.gpsimd
        def _(pool):
            pool.memset(ones[:, :], 1.0).then_inc(consts_set, 1)
            pool.memset(zeros[:, :], 0.0).then_inc(consts_set, 1)
            pool.memset(eps[:, :], EPS).then_inc(consts_set, 1)
            pool.dma_start(onehot, onehot_d).then_inc(onehot_in, 16)
            pool.dma_start(relb, relb_d).then_inc(onehot_in, 16)
            pool.wait_ge(*taken(U["t5", 7]))
            pool.wait_ge(*taken(U["t5", 6]))
            pool.wait_ge(slot_full[15], 16)
            pool.dma_start(scratch.rearrange("(h p n) -> p h n", h=8, n=512), t5rows).then_inc(t5_stored, 16)

            pool.dma_start(poolA, poolA_d).then_inc(pool_in, 16)
            pool.dma_start(poolw, poolw_d).then_inc(pool_in, 16)
            pool.wait_ge(t5_stored, 16)
            pool.wait_ge(s_rope_act, 3)
            pool.dma_start(bias[:, :, 0:HALF],
                           bass.AP(scratch.tensor, 255, [[511, P], [P * 512, 8], [1, HALF]])).then_inc(bias_in, 16)
            pool.dma_start(bias[:, :, HALF:TRI],
                           bass.AP(scratch.tensor, 127, [[511, P], [P * 512, 8], [1, T]])).then_inc(bias_in, 16)
            pool.dma_start(cond[:, 1, :], cond_d[1:2, :].broadcast_to([P, D])).then_inc(cond_in[1], 16)

            def ada_load(v, i=0):
                if not (isinstance(i, int) and v + 8 * i < 2):
                    pool.wait_ge(s_ada, 2 * v - 2 + 16 * i)
                pool.dma_start(ada_slot[:, v % 2, :],
                               ada[bass.ds(v + 8 * i, 1)].rearrange("a p r n -> p (a r n)")).then_inc(ada_full[v % 2], 16)

            for v in range(16):
                ada_load(v)
            for n in range(2):
                with pool.Fori(0, 3) as third:
                    for k in range(8):
                        ada_load(16 + 24 * n + k, third)
                if n == 0:
                    pool.wait_ge(s_h, 24)
                    pool.dma_start(sel, sel_d).then_inc(sel_in, 16)

        @block.tensor
        def _(pe):
            def begin(u):
                if u.nth:
                    pe.wait_ge(freed[u.bank], u.nth)

            def slot_in(pos):
                pe.wait_ge(slot_full[pos % RING], 16 * fills(pos))

            def project(u, moving=h, k0=0, kn=KC, a=0, r=None):
                s = u.pos % RING
                slot_in(u.pos)
                for kc in range(kn):
                    if r is not None:
                        pe.wait_ge(s_h, 8 * r + kc + 1)
                    last = pe.matmul(bank(u, a, a + T), ring[:, s, (k0 + kc) * P:(k0 + kc + 1) * P], moving[:, kc, :],
                                     start=(kc == 0), stop=(kc == kn - 1))
                return last

            def feature_units(name, n, moving=h):
                for c in range(n):
                    u = U[name, c]
                    begin(u)
                    project(u, moving).then_inc(slot_used[u.pos % RING], 1)

            def one(name, moving=h, r=None):
                u = U[name]
                begin(u)
                project(u, moving, r=r).then_inc(slot_used[u.pos % RING], 1)

            def token_unit(u, tile, slots, width, at=0, release=True, do_begin=True):
                if do_begin:
                    begin(u)
                per = KC // slots
                for kc in range(KC):
                    s = (u.pos + kc // per) % RING
                    if kc % per == 0:
                        slot_in(u.pos + kc // per)
                    last = pe.matmul(bank(u, at, at + width), h[:, kc, tile * P:(tile + 1) * P],
                                     ring[:, s, (kc % per) * width:(kc % per + 1) * width],
                                     start=(kc == 0), stop=(kc == KC - 1))
                    if release and kc % per == per - 1:
                        last.then_inc(slot_used[s], 1)
                return last

            def few_outputs(name, r):
                u = U[name]
                begin(u)
                for kc in range(KC):
                    pe.wait_ge(s_h, 8 * r + kc + 1)
                    last = pe.matmul(bank(u, 0, T, 8), col(name, 8 * kc, 8 * kc + 8), h[:, kc, :],
                                     start=(kc == 0), stop=(kc == KC - 1))
                last.then_inc(aux_done, 1)

            def few_per_token(name):
                pe.wait_ge(*taken(U[name]))
                u = U[name + "T"]
                begin(u)
                for tile in range(2):
                    last = pe.transpose(bank(u, 8 * tile, 8 * tile + 8), few[:, tile * P:(tile + 1) * P], ident[0:8, 0:8])
                last.then_inc(aux_done, 1)

            def norm_chunk(r, c):
                pe.wait_ge(s_sq, 8 * r + c + 1)
                ins = pe.matmul(banks[:, norm_bank(r)[0], 0:T], ones[:, :], h[:, c, :], start=(c == 0), stop=(c == KC - 1))
                if c == KC - 1:
                    ins.then_inc(norm_bank(r)[1][0], 1)

            def norm_sum(r):
                if ("stat", r) in U:
                    begin(U["stat", r])
                for c in range(KC):
                    norm_chunk(r, c)

            def out_units(name, r, moving):
                for c in range(KC):
                    u = U[name, c]
                    begin(u)
                    project(u, moving).then_inc(slot_used[u.pos % RING], 1)
                    if c >= 2:
                        norm_chunk(r, c - 2)
                norm_chunk(r, KC - 2)
                norm_chunk(r, KC - 1)

            def rotate(r, moving, ready):
                u = U["rot", r]
                begin(u)
                pe.wait_ge(*ready)
                pe.matmul(bank(u, 0, T), mat("rotate"), moving, start=True, stop=True).then_inc(aux_done, 1)

            def scores(a):
                b = 2 + a.n % 2
                if a.n >= 2:
                    pe.wait_ge(s_logit, 2 * a.n - 2)
                fox = a.kind == "fox"
                last = None
                for lo, hi, q in ((0, HALF, a.q[:, 0:HALF]), (HALF, TRI, a.q[:, HALF:T])):
                    n = hi - lo
                    last = pe.matmul(banks[:, b, lo:hi], q, a.k[:, 0:n], start=True, stop=not fox)
                    if fox:
                        qs = slice(0, HALF) if lo == 0 else slice(HALF, T)
                        last = pe.matmul(banks[:, b, lo:hi], cum[:, qs], sel[:, a.i, 0:n], start=False, stop=True)
                last.then_inc(s_score, 1)

            def transposes(a):
                b = 4 + a.n % 2
                pe.wait_ge(s_prob, 2 * a.n + 2)
                if a.n >= 2:
                    pe.wait_ge(s_pt, a.n - 1)
                for j in range(3):
                    last = pe.transpose(banks[:, b, j * P:(j + 1) * P], logit[:, a.n % (LAG + 1), j * P:(j + 1) * P], ident)
                last.then_inc(s_tr, 1)

            def values(a):
                rows = slice(64 * a.half, 64 * a.half + 64)
                pair = a.n // 2
                at = (pair % 2) * T
                pe.wait_ge(s_pt, a.n + 1)
                if pair >= 1 and a.half == 0:
                    pe.wait_ge(s_o, pair)
                pe.matmul(banks[rows, 6, at:at + T], a.v[:, 0, a.vcol:a.vcol + 64], probT[:, a.n % 2, 0:T],
                          start=True, stop=False)
                pe.matmul(banks[rows, 6, at + HALF:at + T], a.v[:, 1, a.vcol:a.vcol + 64], probT[:, a.n % 2, T:TRI],
                          start=False, stop=True).then_inc(s_pv, 1)

            def attend(heads, between):
                for i in range(len(heads) + LAG + 1):
                    if i < len(heads):
                        scores(heads[i])
                    for step in between.get(i, ()):
                        step()
                    if 0 <= i - LAG < len(heads):
                        transposes(heads[i - LAG])
                    if i > LAG:
                        values(heads[i - LAG - 1])

            def out_open():
                pe.wait_ge(consts_set, 2)
                for b in range(4, 8):
                    pe.matmul(banks[:, b, :], zeros[:, :], finite, start=True, stop=False,
                              skip_group_check=True)

            def out_close(b):
                pe.matmul(banks[:, b, :], zeros[:, :], finite, start=False, stop=True,
                          skip_group_check=True).then_inc(s_acc, 1)

            def ffn(name, r0):
                u0 = U[name]
                pe.wait_ge(*norm_bank(r0)[2])
                out_open()

                def down(i, j, final=False):
                    pos = u0.pos + 3 * j + 2
                    s = pos % RING
                    pe.wait_ge(slot_full[s], 16 * (fills(pos) + i))
                    pe.wait_ge(freed[j % 2], u0.nth[j % 2] + (BODY // 2) * i + j // 2 + 1)
                    for c in range(KC):
                        last = pe.matmul(banks[:, 4 + c // 2, (c % 2) * T:(c % 2 + 1) * T],
                                         ring[:, s, c * P:(c + 1) * P], hid[:, j % 2, :],
                                         start=False, stop=False, skip_group_check=True)
                        if c == KC - 1:
                            last.then_inc(slot_used[s], 1)
                        if final and c % 2:
                            out_close(4 + c // 2)

                def up(i, j, first=False):
                    b = j % 2
                    pe.wait_ge(freed[b], u0.nth[b] + (BODY // 2) * i + j // 2)
                    for r in range(2):
                        pos = u0.pos + 3 * j + r
                        s = pos % RING
                        pe.wait_ge(slot_full[s], 16 * (fills(pos) + i))
                        for kc in range(KC):
                            if first and r == 0:
                                pe.wait_ge(s_h, 8 * r0 + kc + 1)
                            last = pe.matmul(banks[:, b, r * T:(r + 1) * T], ring[:, s, kc * P:(kc + 1) * P], h[:, kc, :],
                                             start=(kc == 0), stop=(kc == KC - 1))
                        last.then_inc(slot_used[s], 1)

                up(0, 0, True)
                with pe.Fori(0, TURNS) as i:
                    for j in range(BODY):
                        up(i, j + 1)
                        down(i, j)
                rest = FC - TURNS * BODY
                for j in range(rest - 1):
                    up(TURNS, j + 1)
                    down(TURNS, j)
                down(TURNS, rest - 1, True)

            pe.wait_ge(consts_set, 1)
            norm_sum(0)
            pe.wait_ge(onehot_in, 32)
            for i in range(8):
                u = U["t5", i]
                begin(u)
                pe.matmul(bank(u), relb[:, i, :], onehot, start=True, stop=True).then_inc(aux_done, 1)

            def qkstat(j):
                u = U["qkstat", j]
                begin(u)
                for e in range(2):
                    c = 2 * j + e
                    pe.wait_ge(s_qksq, c + 1)
                    last = pe.matmul(bank(u, e * T, (e + 1) * T), mat("heads"), qksq[:, c % 4, :], start=True, stop=True)
                last.then_inc(aux_done, 1)

            one(("q", 0), r=0)
            for c in range(1, 4):
                one(("q", c))
            pe.wait_ge(mats_in, 16)
            qkstat(0)
            one(("k", 0))
            one(("k", 1))
            qkstat(1)
            one(("k", 2))
            one(("k", 3))
            qkstat(2)
            token_unit(U["v", 0], 0, 4, 512, release=False).then_inc(aux_done, 1)
            token_unit(U["v", 1], 1, 4, 512)
            qkstat(3)
            token_unit(U["p", 0], 0, 4, 512, release=False).then_inc(aux_done, 1)
            token_unit(U["p", 1], 1, 4, 512)
            pe.wait_ge(pool_in, 32)
            pe.wait_ge(*taken(U["p", 0]))
            pe.wait_ge(*taken(U["p", 1]))
            for g2 in range(2):
                u = U["pool", g2]
                begin(u)
                for e in range(2):
                    g = 2 * g2 + e
                    pe.matmul(bank(u, e * T, (e + 1) * T), p_tok[:, 0, g * P:(g + 1) * P], poolA[:, 0, g, :],
                              start=True, stop=False)
                    last = pe.matmul(bank(u, e * T + HALF, (e + 1) * T), p_tok[:, 1, g * P:(g + 1) * P],
                                     poolA[:, 1, g, HALF:T], start=False, stop=True)
                last.then_inc(aux_done, 1)
            for g2 in range(2):
                u = U["poolw", g2]
                begin(u)
                pe.wait_ge(*taken(U["pool", g2]))
                for e in range(2):
                    g = 2 * g2 + e
                    last = pe.matmul(bank(u, e * T, (e + 1) * T), poolw[:, g, :], poolT[:, g, :], start=True, stop=True)
                last.then_inc(aux_done, 1)
            pe.wait_ge(s_qk, 8)
            pe.wait_ge(*taken(U["v", 0]))
            pe.wait_ge(*taken(U["v", 1]))
            gates = [("ga", c) for c in range(8)] + [("gp", c) for c in range(8)]
            between = {i: [lambda g=g: one(g) for g in gates[2 * i:2 * i + 2]] for i in range(8)}
            attend(first_heads, between)
            pe.wait_ge(s_o, 4)
            pe.wait_ge(*taken(U["poolw", 0]))
            pe.wait_ge(*taken(U["poolw", 1]))
            for c in range(8):
                u = U["br", c]
                begin(u)
                project(u, oT1, 0, 4, 0)
                project(u, pool2, 4, 4, T).then_inc(slot_used[u.pos % RING], 1)
            pe.wait_ge(s_merged, 16)
            out_units("wo", 1, merged)
            ffn("ffn1", 1)
            norm_sum(2)
            few_outputs("fgl", 2)
            one(("fq", 0))
            few_per_token("fgl")
            for c in range(1, 4):
                one(("fq", c))
            feature_units("fk", 4)
            u = U["cum"]
            begin(u)
            pe.wait_ge(s_forget, 7)
            pe.matmul(banks[0:72, u.bank, 0:T], lf72[:, 0, :], upto, start=True, stop=False)
            pe.matmul(banks[0:72, u.bank, HALF:T], lf72[:, 1, :], upto[:, 0:HALF], start=False, stop=True).then_inc(aux_done, 1)
            token_unit(U["fv", 0], 0, 4, 512, release=False).then_inc(aux_done, 1)
            token_unit(U["fv", 1], 1, 4, 512)
            pe.wait_ge(s_cum, 3)
            for name in ("fk", 3), ("fk", 2), "cum", ("fv", 0), ("fv", 1):
                pe.wait_ge(*taken(U[name]))

            def sv_unit():
                u = U["sv"]
                token_unit(u, 0, 1, P, 0, release=False)
                token_unit(u, 1, 1, P, P, do_begin=False)

            def rot_of(r, name, c, tile):
                return lambda: rotate(r, tile, taken(U[name, c]))

            def swa_ready():
                pe.wait_ge(s_rope, 5)
                pe.wait_ge(*taken(U["sv"]))

            between = {0: [lambda: one(("sq", 0))],
                       1: [lambda: one(("sq", 1)), rot_of(0, "sq", 0, sqT[:, 0])],
                       2: [lambda: one(("sq", 2)), rot_of(1, "sq", 1, sqT[:, 1])],
                       3: [lambda: one(("sq", 3)), rot_of(2, "sq", 2, sqT[:, 2])],
                       4: [lambda: one(("sk", 0)), rot_of(3, "sq", 3, sqT[:, 3])],
                       5: [sv_unit, rot_of(4, "sk", 0, skT)],
                       7: [swa_ready]}
            attend(even_heads, between)
            pe.wait_ge(s_o, 12)
            out_units("eo", 3, oT2)
            ffn("ffn2", 3)
            norm_sum(4)
            few_outputs("iw", 4)
            one(("ik", 0))
            few_per_token("iw")
            for c in range(4):
                one(("iq", c))
                rotate(5 + c, *((ikT, taken(U["ik", 0])) if c == 0 else (iqT[:, c - 1], taken(U["iq", c - 1]))))
            one(("dk", 0))
            rotate(9, iqT[:, 3], taken(U["iq", 3]))
            one(("dk", 1))
            for m in range(8):
                pe.wait_ge(s_rope, 7 + m // 2)
                if m == 0:
                    pe.wait_ge(s_logit, 48)
                if m >= 2:
                    pe.wait_ge(s_relu, m - 1)
                rows = slice(64 * (m % 2), 64 * (m % 2) + 64)
                pe.matmul(banks[:, 2 + m % 2, 0:HALF], iqT[rows, m // 2, 0:HALF], ikT[rows, 0:HALF], start=True, stop=True)
                pe.matmul(banks[:, 2 + m % 2, HALF:TRI], iqT[rows, m // 2, HALF:T], ikT[rows, :], start=True, stop=True)\
                  .then_inc(s_iscore, 1)
            rotate(10, dkT[:, 0], taken(U["dk", 0]))
            u = U["dv"]
            token_unit(u, 0, 2, T, 0, release=False)
            token_unit(u, 1, 2, T, T, do_begin=False)
            rotate(11, dkT[:, 1], taken(U["dk", 1]))
            one(("dq", 0))

            def dq(c):
                def step():
                    if c < 8:
                        one(("dq", c))
                    rotate(11 + c, dqT[:, c - 1], taken(U["dq", c - 1]))
                return step

            for c in range(1, 4):
                dq(c)()
            pe.wait_ge(*taken(U["dv"]))
            pe.wait_ge(s_relu, 8)
            between = {}
            for c in range(4, 9):
                between[2 * (c - 4)] = between.get(2 * (c - 4), []) + [dq(c)]
            for c in range(1, 8):
                between.setdefault(2 * c - 1, []).append(lambda c=c: pe.wait_ge(s_rope, 13 + c))
            pe.wait_ge(s_rope, 13)
            attend(odd_heads, between)
            pe.wait_ge(s_o, 20)
            out_units("oo", 5, dqT)
            few_outputs("router", 5)

            def token_chunks(t):
                u = U["htok", t]
                begin(u)
                for j in range(4):
                    last = pe.transpose(bank(u, j * P, (j + 1) * P), h[:, 4 * (t % 2) + j, (t // 2) * P:(t // 2 + 1) * P], ident)
                last.then_inc(aux_done, 1)

            token_chunks(0)
            token_chunks(1)
            few_per_token("router")
            token_chunks(2)
            token_chunks(3)
            u = U["ranks"]
            begin(u)
            pe.wait_ge(s_route, 9)
            picked = rt[:, 0:16].rearrange("p (a e) -> p a e", a=2)
            pe.matmul(bank(u, 0, 8), upto[:, 0:HALF], picked[:, 0, :], start=True, stop=True)
            pe.matmul(bank(u, 8, 16), ones[:, :], picked[:, 0, :], start=True, stop=False)
            pe.matmul(bank(u, 8, 16), upto[:, 0:HALF], picked[:, 1, :], start=False, stop=True)
            pe.matmul(bank(u, 16, 24), ones[:, :], picked[:, 0, :], start=True, stop=False)
            pe.matmul(bank(u, 16, 24), ones[:, :], picked[:, 1, :], start=False, stop=True).then_inc(aux_done, 1)
            def gather(b, half):
                for j in range(4):
                    c = 4 * half + j
                    for tile in range(2):
                        last = pe.matmul(banks[:, b, j * CAP:(j + 1) * CAP], htok[:, tile, c * P:(c + 1) * P], pick[:, tile, :],
                                         start=(tile == 0), stop=(tile == 1))
                last.then_inc(aux_done, 1)

            for t in range(2, 4):
                pe.wait_ge(*taken(U["htok", t]))
            for half in range(2):
                begin(U["gather", half])
                pe.wait_ge(s_pick, 2)
                gather(U["gather", half].bank, half)
            m0 = U["moe"]
            before = [len(range(s, m0.pos, RING)) if s < RING else 0 for s in range(MSLOTS)]
            out_open()

            def bank_free(p, r):
                pe.wait_ge(freed[r % 2], m0.nth[r % 2] + USES // 2 * p + r // 2)

            def scatter(close=False):
                for c in range(KC):
                    pe.matmul(banks[:, 4 + c // 2, (c % 2) * T:(c % 2 + 1) * T], y_tok[:, c * P:(c + 1) * P], pickT[:, :],
                              start=False, stop=False, skip_group_check=True)
                    if close and c % 2:
                        out_close(4 + c // 2)

            def expert_up(p, f):
                r = use_of(f)
                bank_free(p, r)
                if f == 0:
                    pe.wait_ge(freed[1], m0.nth[1] + USES // 2 * p)
                for e in range(2):
                    m = 3 * f + e
                    pe.wait_ge(slot_full[m], 16 * (before[m] + p + 1))
                    for kc in range(KC):
                        last = pe.matmul(banks[:, r % 2, e * T:e * T + CAP], moe_slot(m)[:, kc * P:(kc + 1) * P], hg[:, kc, :],
                                         start=(kc == 0), stop=(kc == KC - 1))
                    last.then_inc(slot_used[m], 1)

            def expert_down(p, f):
                m = 3 * f + 2
                r = use_of(f)
                pe.wait_ge(slot_full[m], 16 * (before[m] + p + 1))
                pe.wait_ge(freed[r % 2], m0.nth[r % 2] + USES // 2 * p + r // 2 + 1)
                for half in range(2):
                    last = pe.matmul(banks[0:CAP, 2 + half, :], ehid[:, f % 2, :], moe_slot(m)[:, half * 512:(half + 1) * 512],
                                     start=(f == 0), stop=(f == EF - 1))
                last.then_inc(slot_used[m], 1)

            def expert_pass(p, first=False):
                expert_up(p, 0)
                if not first:
                    pe.wait_ge(s_y_act, p)
                    pe.wait_ge(s_y_dve, p)
                    scatter()
                expert_up(p, 1)
                bank_free(p, 2)
                pe.wait_ge(s_cpick, 2 * p + 2)
                for tile in range(2):
                    last = pe.transpose(banks[0:CAP, 0, tile * P:(tile + 1) * P], cpick[:, tile, :], ident)
                last.then_inc(aux_done, 1)
                expert_down(p, 0)
                for f in range(2, EF):
                    expert_up(p, f)
                    if f == EF - 1:
                        pe.wait_ge(s_pick, 2 * p + 4)
                        for half in range(2):
                            bank_free(p, USES - 2 + half)
                            gather(half, half)
                    expert_down(p, f - 1)
                expert_down(p, EF - 1)

            expert_pass(0, True)
            pe.wait_ge(s_passes, 1)
            passes = pe.value_load(ints[0:1, NTAB:NTAB + 1], min_val=EXPERTS, max_val=EXPERTS + EXTRA)
            with pe.Fori(1, passes) as p:
                expert_pass(p)
            pe.wait_ge(s_y_act, passes)
            pe.wait_ge(s_y_dve, passes)
            scatter(True)
            pe.wait_ge(freed[0], m0.nth[0] + USES // 2 * passes)
            norm_sum(6)

        @block.scalar
        def _(act):
            warmed = []

            def take(u, out, a=0, b=512, parts=P, func=ACT.Copy, **k):
                act.wait_ge(*u.done)
                act.activation(out, bank(u, a, b, parts), func, **k).then_inc(freed[u.bank], 1)

            def load_table(func):
                n = len(warmed)
                warmed.append(func)
                act.activation(warm[:, n:n + 1], eps[:, :], func)

            def squares(r):
                if r:
                    load_table(ACT.Sqrt)
                for c in range(KC):
                    if r == 0:
                        if c == 0:
                            act.wait_ge(x_in, 16)
                    else:
                        act.wait_ge(*x_ready(r - 1, c))
                    act.activation(h[:, c, :], x[:, c, :], ACT.Square).then_inc(s_sq, 1)

            def root(r):
                b, done, read = norm_bank(r)
                act.wait_ge(*done)
                act.activation(var[:, 0:T], banks[:, b, 0:T], ACT.Sqrt, scale=1.0 / D, bias=eps[:, :]).then_inc(read[0], 1)

            def scale_shift(r):
                act.wait_ge(s_avec, r + 1)
                third, at = norm_scale_source(r)[0]
                for c in range(KC):
                    act.wait_ge(s_xn, 8 * r + c + 1)
                    act.activation(h[:, c, :], h[:, c, :], ACT.Identity, scale=avec[:, r, c:c + 1],
                                   bias=mod[:, third, at + c:at + c + 1]).then_inc(s_h, 1)

            def norm(r):
                squares(r)
                root(r)
                scale_shift(r)

            def exps(a):
                st, lg = stats[:, a.n % (LAG + 1)], logit[:, a.n % (LAG + 1)]
                sink = a.kind == "swa"
                for j, (lo, hi) in enumerate(((0, HALF), (HALF, TRI))):
                    act.wait_ge(s_logit, 2 * a.n + j + 1)
                    act.activation(lg[:, lo:hi], lg[:, lo:hi], ACT.Exp, scale=-1.0, bias=st[:, j:j + 1],
                                   accum_out=st[:, 2 + j:3 + j]).then_inc(s_exp, 1)
                if sink:
                    act.activation(st[:, 6:8], st[:, 0:2], ACT.Exp,
                                   bias=col("rows", 8 + a.sink, 9 + a.sink)).then_inc(s_exp, 1)

            def attend(heads, between):
                for i in range(len(heads) + LAG + 1):
                    if i < len(heads):
                        exps(heads[i])
                    for step in between.get(i, ()):
                        step()
                    if 0 <= i - LAG < len(heads):
                        a = heads[i - LAG]
                        act.wait_ge(s_tr, a.n + 1)
                        if a.n >= 2:
                            act.wait_ge(s_pv, a.n - 1)
                        act.activation(probT[:, a.n % 2, :], banks[:, 4 + a.n % 2, 0:TRI], ACT.Copy).then_inc(s_pt, 1)
                    if i > LAG and heads[i - LAG - 1].half:
                        a = heads[i - LAG - 1]
                        at = (a.n // 2 % 2) * T
                        act.wait_ge(s_pv, a.n + 1)
                        act.activation(a.out, banks[:, 6, at:at + T], ACT.Copy).then_inc(s_o, 1)

            def ffn(name, conv):
                u0 = U[name]

                def chunk(i, j):
                    b = j % 2
                    f = BODY * i + j
                    up = u0.pos + 3 * j + 1
                    act.wait_ge(slot_used[up % RING], fills(up) + i)
                    if not conv:
                        act.activation(sg[:, b, :], banks[:, b, 0:T], ACT.Silu).then_inc(s_silu, 1)
                        return
                    if j == 0:
                        act.wait_ge(s_taps_in, i + 1)
                    act.activation(yg[:, b, :], banks[:, b, 0:T], ACT.Identity, scale=taps[:, j, 2:3],
                                   bias=taps[:, j, 3:4]).then_inc(s_conv, 1)
                    act.activation(yv[:, b, :], banks[:, b, T:2 * T], ACT.Identity, scale=taps[:, j, 6:7],
                                   bias=taps[:, j, 7:8]).then_inc(s_conv, 1)
                    act.wait_ge(s_tap, 4 * f + 3)
                    act.activation(sg[:, b, :], yg[:, b, :], ACT.Silu).then_inc(s_silu, 1)

                if conv:
                    act.nop().then_inc(s_conv, 1)
                with act.Fori(0, TURNS) as i:
                    for j in range(BODY):
                        chunk(i, j)
                for j in range(FC - TURNS * BODY):
                    chunk(TURNS, j)

            def condition(n):
                act.wait_ge(cond_in[n], 16)
                act.activation(cond[:, n, :], cond[:, n, :], ACT.Silu).then_inc(s_cact, 1)

            condition(0)
            squares(0)
            act.wait_ge(consts_set, 3)
            root(0)
            for i in range(8):
                take(U["t5", i], t5rows[:, i, :], scale=1 / SCALE)
            act.wait_ge(s_rope_dve, 9)
            act.activation(sin[:, :], ang, ACT.Sin).then_inc(s_rope_act, 1)
            act.activation(turns, ang, ACT.Abs).then_inc(s_rope_act, 1)
            act.wait_ge(s_rope_act, 2)
            act.wait_ge(s_rope_dve, 10)
            act.activation(cos[:, :], turns, ACT.Sin, scale=-1.0, bias=half_pi[:, :]).then_inc(s_rope_act, 1)
            scale_shift(0)
            act.wait_ge(s_rope_act, 3)

            def take_qk(c):
                u = U[("q", "k")[c // 4], c % 4]
                act.wait_ge(*u.done)
                if c >= 4:
                    act.wait_ge(*U["qkstat", (c - 4) // 2].done)
                act.activation(qksq[:, c % 4, :], bank(u, 0, T), ACT.Square).then_inc(s_qksq, 1)
                act.activation((qT, kT)[c // 4][:, c % 4, :], bank(u, 0, T), ACT.Copy).then_inc(freed[u.bank], 1)

            def qk_root(j):
                u = U["qkstat", j]
                act.wait_ge(*u.done)
                if j:
                    act.wait_ge(s_qk, 2 * j)
                act.activation(var[:, :], bank(u), ACT.Sqrt, scale=1.0 / HD, bias=eps[:, :]).then_inc(freed[u.bank], 1)

            for c in range(4):
                take_qk(c)
            qk_root(0)
            for j in range(1, 3):
                take_qk(2 * j + 2)
                take_qk(2 * j + 3)
                qk_root(j)
            take(U["v", 0], v_tok[:, 0, :])
            take(U["v", 1], v_tok[:, 1, :])
            qk_root(3)
            take(U["p", 0], p_tok[:, 0, :])
            take(U["p", 1], p_tok[:, 1, :])
            condition(1)
            for g in range(2):
                take(U["pool", g], poolT[:, 2 * g:2 * g + 2, :].rearrange("p a t -> p (a t)"))
            for g2 in range(2):
                u = U["poolw", g2]
                act.wait_ge(*u.done)
                for e in range(2):
                    g = 2 * g2 + e
                    ins = act.activation(pool2[:, g, :], bank(u, e * T, (e + 1) * T), ACT.Copy,
                                         scale=col("pool_scale", g, g + 1))
                    ins.then_inc(*((freed[u.bank], 1) if e else (s_pool, 1)))
            gates = [("ga", c) for c in range(8)] + [("gp", c) for c in range(8)]

            def take_gate(g):
                take(U[g], (ga if g[0] == "ga" else gp)[:, g[1], :], 0, T, func=ACT.Tanh, scale=0.5)

            attend(first_heads, {i: [lambda g=g: take_gate(g) for g in gates[2 * i:2 * i + 2]] for i in range(8)})
            norm(1)
            ffn("ffn1", True)
            norm(2)
            take(U["fgl"], few, 0, T, 8)
            take(U["fq", 0], fqT[:, 0, :], 0, T)
            take(U["fq", 1], fqT[:, 1, :], 0, T)
            act.wait_ge(s_forget, 1)
            act.wait_ge(*taken(U["fglT"]))
            flat = lf.rearrange("p a b c -> p a (b c)")
            act.activation(flat[:, 1], flat[:, 0], ACT.Abs).then_inc(s_forget, 1)
            act.wait_ge(s_forget, 2)
            act.activation(flat[:, 1], flat[:, 1], ACT.Exp, scale=-1.0).then_inc(s_forget, 1)
            act.wait_ge(s_forget, 3)
            act.activation(flat[:, 1], flat[:, 1], ACT.Ln, bias=1.0).then_inc(s_forget, 1)
            for c in range(2, 4):
                take(U["fq", c], fqT[:, c, :], 0, T)
            for c in range(4):
                take(U["fk", c], fkT[:, c, :], 0, T)
            take(U["fv", 0], fv[:, 0, :])
            take(U["fv", 1], fv[:, 1, :])
            between = {c: [lambda c=c: take(U["sq", c], sqT[:, c, :], 0, T)] for c in range(4)}
            between[4] = [lambda: take(U["sk", 0], skT, 0, T)]
            between[5] = [lambda: take(U["sv"], sv.rearrange("p a n -> p (a n)"), 0, T)]
            attend(even_heads, between)
            norm(3)
            ffn("ffn2", False)
            norm(4)
            take(U["iw"], few, 0, T, 8)
            take(U["ik", 0], ikT, 0, T)
            take(U["iwT"], iws.rearrange("p a n -> p (a n)"), 0, 16, scale=float(8 ** -0.5 * 64 ** -0.5))
            for c in range(4):
                take(U["iq", c], iqT[:, c, :], 0, T)
            for c in range(2):
                take(U["dk", c], dkT[:, c, :], 0, T)
            for m in range(8):
                act.wait_ge(s_iscore, m + 1)
                if m >= 2:
                    act.wait_ge(s_isum, 2 * m - 2)
                act.activation(relu[:, m % 2, :], banks[:, 2 + m % 2, 0:TRI], ACT.Relu).then_inc(s_relu, 1)
            take(U["dv"], dv.rearrange("p a n -> p (a n)"))
            for c in range(4):
                take(U["dq", c], dqT[:, c, :], 0, T)
            attend(odd_heads, {2 * (c - 4): [lambda c=c: take(U["dq", c], dqT[:, c, :], 0, T)] for c in range(4, 8)})
            norm(5)
            load_table(ACT.Exp)
            take(U["router"], few, 0, T, 8)
            for t in range(4):
                take(U["htok", t], htok[:, t // 2, (t % 2) * 512:(t % 2 + 1) * 512])
            act.wait_ge(s_route, 11)
            lg = rt[:, 112:128]
            act.activation(lg, lg, ACT.Exp).then_inc(s_gexp, 1)
            for half in range(2):
                take(U["gather", half], hg[:, 4 * half:4 * half + 4, :].rearrange("p a n -> p (a n)"), 0, 4 * CAP)
            m0 = U["moe"]
            before = [len(range(s, m0.pos, RING)) if s < RING else 0 for s in range(MSLOTS)]
            def expert_pass(p):
                for f in range(EF):
                    act.wait_ge(slot_used[3 * f + 1], before[3 * f + 1] + p + 1)
                    act.activation(esg[:, f % 2, :], banks[:, use_of(f) % 2, 0:CAP], ACT.Silu).then_inc(s_silu, 1)
                act.wait_ge(aux_done, m0.done + 3 * p + 3)
                act.activation(hg[:, 4:8, :].rearrange("p a n -> p (a n)"), banks[:, 1, 0:4 * CAP], ACT.Copy).then_inc(freed[1], 1)
                act.wait_ge(slot_used[MSLOTS - 1], before[MSLOTS - 1] + p + 1)
                act.activation(y_tok[:, 0:512], banks[0:CAP, 2, :], ACT.Copy).then_inc(s_y_act, 1)

            expert_pass(0)
            act.wait_ge(s_passes, 1)
            passes = act.value_load(ints[0:1, NTAB:NTAB + 1], min_val=EXPERTS, max_val=EXPERTS + EXTRA)
            with act.Fori(1, passes) as p:
                expert_pass(p)
            squares(6)
            root(6)
            for c in range(KC):
                act.wait_ge(s_xn, 48 + c + 1)
                act.activation(h[:, c, :], h[:, c, :], ACT.Identity, scale=col("final_norm", c, c + 1)).then_inc(s_final, 1)

        @block.vector
        def _(dve):
            def norm(r):
                norm_root(r)
                norm_chunks(r, 0, KC)

            def norm_root(r):
                b, done, read = norm_bank(r)
                dve.wait_ge(*read)
                dve.reciprocal(rstd, var[:, 0:T]).then_inc(s_rstd, 1)
                dve.wait_ge(s_rstd, r + 1)

            def norm_chunks(r, c0, c1):
                for c in range(c0, c1):
                    ins = dve.tensor_tensor(h[:, c, :], x[:, c, :], rstd, ALU.mult)
                    ins.then_inc(s_xn, 1)

            def ada_column(n, layer0, weights, inc):
                dve.tensor_tensor_reduce(weights, weights, cond[:, 0 if layer0 else 1, :], 1.0, 0.0, ALU.mult, ALU.add,
                                         accum_out=msum[:, n:n + 1]).then_inc(*inc)

            def ada_unit(third, k, i=0):
                v = 8 * (third - 1) + k
                dve.wait_ge(ada_full[v % 2], 16 * (v // 2 + 1) + 64 * i)
                if k == 0:
                    dve.wait_ge(s_mod, third + i)
                    if third == 3:
                        dve.wait_ge(s_cact, 2)
                for half in range(2):
                    ada_column(2 * k + half, third < 3, ada_slot[:, v % 2, half * SLOT:(half + 1) * SLOT], (s_ada, 1))

            def modulation(third, name, i=0):
                if third:
                    dve.wait_ge(s_ada, 16 * (third + i))
                else:
                    dve.wait_ge(slot_used[15], 1)
                n = third % 3
                if isinstance(i, int):
                    dve.tensor_tensor(mod[:, third + i, :], msum[:, :], col(name, 16 * (n + i), 16 * (n + i) + 16), ALU.add)\
                       .then_inc(s_mod, 1)
                else:
                    at = COLS[name][0]
                    dve.tensor_tensor(mod[:, bass.ds(third + i, 1), :].rearrange("p a n -> p (a n)"), msum[:, :],
                                      cols[:, bass.ds(at + 16 * i, 16)], ALU.add).then_inc(s_mod, 1)

            def norm_vector(r):
                third, at = norm_scale_source(r)[1]
                dve.wait_ge(s_mod, third + 1)
                dve.scalar_tensor_tensor(avec[:, r, :], mod[:, third, at:at + 8], 1.0, col(NORM_GAINS[r]),
                                         ALU.add, ALU.mult).then_inc(s_avec, 1)

            def softmax_start(a):
                st, lg = stats[:, a.n % (LAG + 1)], logit[:, a.n % (LAG + 1)]
                sink = a.kind == "swa"
                dve.wait_ge(s_score, a.n + 1)
                if a.n > LAG:
                    dve.wait_ge(s_tr, a.n - LAG)
                first = negsink[:, a.sink:a.sink + 1] if sink else -TAKEN
                for j, (lo, hi) in enumerate(((0, HALF), (HALF, TRI))):
                    dve.tensor_tensor_reduce(lg[:, lo:hi], banks[:, 2 + a.n % 2, lo:hi], a.bias[:, lo:hi], -SCALE, first,
                                             ALU.add, ALU.min, accum_out=st[:, j:j + 1]).then_inc(s_logit, 1)

            def softmax_end(a):
                st, lg = stats[:, a.n % (LAG + 1)], logit[:, a.n % (LAG + 1)]
                dve.wait_ge(s_exp, exp_count(a.n))
                if a.kind == "swa":
                    dve.tensor_tensor(st[:, 2:4], st[:, 2:4], st[:, 6:8], ALU.add).then_inc(s_rsum, 1)
                    dve.wait_ge(s_rsum, rsum_count(a.n) - 1)
                dve.reciprocal(st[:, 4:6], st[:, 2:4]).then_inc(s_rsum, 1)
                dve.wait_ge(s_rsum, rsum_count(a.n))
                for j, (lo, hi) in enumerate(((0, HALF), (HALF, TRI))):
                    dve.tensor_scalar(lg[:, lo:hi], lg[:, lo:hi], st[:, 4 + j:5 + j], None, ALU.mult).then_inc(s_prob, 1)

            def attend(heads, between):
                for i in range(len(heads) + 1):
                    if i < len(heads):
                        softmax_start(heads[i])
                    if i >= 1:
                        softmax_end(heads[i - 1])
                    for step in between.get(i, ()):
                        step()

            def rope(r, tile, raw):
                u = U["rot", r]
                dve.wait_ge(*u.done)
                dve.tensor_tensor(ropet[:, r % 2, :], bank(u, 0, T), sin[:, :], ALU.mult).then_inc(freed[u.bank], 1)
                dve.wait_ge(*taken(U[raw]))
                dve.tensor_tensor(tile, tile, cos[:, :], ALU.mult).then_inc(s_rot, 1)
                dve.wait_ge(s_rot, r + 1)
                dve.wait_ge(*taken(u))
                dve.tensor_tensor(tile, tile, ropet[:, r % 2, :], ALU.add).then_inc(s_rope, 1)

            def residual_units(name, gate, between={}):
                for c in range(KC):
                    if c in between:
                        between[c]()
                    u = U[name, c]
                    dve.wait_ge(*u.done)
                    dve.scalar_tensor_tensor(x[:, c, :], bank(u, 0, T), gate[:, c:c + 1], x[:, c, :], ALU.mult, ALU.add)\
                       .then_inc(freed[u.bank], 1)

            def residual_acc(layer):
                for c in range(KC):
                    dve.wait_ge(s_acc, 4 * layer + c // 2 + 1)
                    dve.scalar_tensor_tensor(x[:, c, :], banks[:, 4 + c // 2, (c % 2) * T:(c % 2 + 1) * T],
                                             mod[:, 3 * layer + 2, 8 + c:9 + c], x[:, c, :], ALU.mult, ALU.add).then_inc(s_x, 1)

            def ffn(name, conv, third0, ada_b):
                u0 = U[name]
                f0 = 0 if conv else FC

                def chunk(i, j, units):
                    b = j % 2
                    f = BODY * i + j
                    up = u0.pos + 3 * j + 1
                    if conv:
                        if j == 0:
                            if not (isinstance(i, int) and i == 0):
                                dve.wait_ge(s_conv, 2 * BODY * i + 1)
                            at = COLS["conv"][0]
                            n = 8 * BODY if not isinstance(i, int) else 8 * (FC - TURNS * BODY)
                            source = cols[:, bass.ds(at + 8 * BODY * i, n)]
                            dve.tensor_copy(taps.rearrange("p a b -> p (a b)")[:, 0:n], source).then_inc(s_taps_in, 1)
                            dve.wait_ge(s_taps_in, i + 1)
                        for tap in (1, 0):
                            for e, y in ((0, yg), (1, yv)):
                                if tap == 1:
                                    dve.wait_ge(s_conv, 2 * f + 3)
                                else:
                                    dve.wait_ge(s_tap, 4 * f + e + 1)
                                lag = 2 - tap
                                dve.scalar_tensor_tensor(y[:, b, lag:T], banks[:, b, e * T:(e + 1) * T - lag],
                                                         taps[:, j, 4 * e + tap:4 * e + tap + 1], y[:, b, lag:T],
                                                         ALU.mult, ALU.add).then_inc(s_tap, 1)
                    dve.wait_ge(s_silu, f0 + f + 1)
                    if conv:
                        dve.wait_ge(s_tap, 4 * f + 4)
                        dve.tensor_tensor(hid[:, b, :], sg[:, b, :], yv[:, b, :], ALU.mult).then_inc(freed[b], 1)
                    else:
                        dve.wait_ge(slot_used[up % RING], fills(up) + i)
                        dve.tensor_tensor(hid[:, b, :], sg[:, b, :], banks[:, b, T:2 * T], ALU.mult).then_inc(freed[b], 1)
                    for k in units:
                        ada_unit(third0, k, i)

                with dve.Fori(0, TURNS) as i:
                    for j in range(BODY):
                        chunk(i, j, [j])
                    modulation(third0, ada_b, i)
                for j in range(FC - TURNS * BODY):
                    chunk(TURNS, j, ([0, 1], [2, 3], [4, 5], [6], [7], [])[j])
                residual_acc(third0 // 3 - 1)
                modulation(third0 + TURNS, ada_b)
                norm_vector(2 * third0 // 3)
                norm_vector(2 * third0 // 3 + 1)

            dve.wait_ge(pos_in, 16)
            dve.wait_ge(cols_in, 16)
            chain = [0]

            def link(ins, s):
                chain[0] += 1
                ins.then_inc(s, 1)
                dve.wait_ge(s, chain[0])

            link(dve.tensor_copy(posf, posi), s_rope_dve)
            link(dve.tensor_scalar(ang, posf, col("inv_freq"), None, ALU.mult), s_rope_dve)
            link(dve.tensor_scalar(turns, ang, float(1 / (2 * np.pi)), MAGIC, ALU.mult, ALU.add), s_rope_dve)
            link(dve.tensor_scalar(turns, turns, MAGIC, None, ALU.subtract), s_rope_dve)
            for part in TWO_PI_PARTS:
                link(dve.scalar_tensor_tensor(ang, turns, -part, ang, ALU.mult, ALU.add), s_rope_dve)
            link(dve.tensor_scalar(ang, ang, PI_CLAMP, -PI_CLAMP, ALU.min, ALU.max), s_rope_dve)
            link(dve.memset(half_pi[:, :], float(np.pi / 2)), s_rope_dve)
            link(dve.tensor_scalar(negsink[:, :], col("rows", 8, 16), -1.0, None, ALU.mult), s_rope_dve)
            dve.wait_ge(s_cact, 1)
            for kc in range(KC):
                for s in (2 * kc, 2 * kc + 1):
                    dve.wait_ge(slot_full[s], 16)
                    ada_column(s, True, ring[:, s, :], (slot_used[s], 1))
                if kc == 3:
                    norm_root(0)
                if kc >= 4:
                    norm_chunks(0, 2 * (kc - 4), 2 * (kc - 4) + 2)
            modulation(0, "ada_b")
            norm_vector(0)
            dve.wait_ge(s_xn, 8)
            for j in range(4):
                u = U["qkstat", j]
                dve.wait_ge(*taken(u))
                dve.reciprocal(var[:, :], var[:, :]).then_inc(s_qkrstd, 1)
                dve.wait_ge(s_qkrstd, j + 1)
                for e in range(2):
                    c = 2 * j + e
                    tile = (qT, kT)[c // 4][:, c % 4, :]
                    dve.wait_ge(*taken(U[("q", "k")[c // 4], c % 4]))
                    dve.scalar_tensor_tensor(tile, tile, col(("q_norm_g", "k_norm_g")[c // 4]), var[:, e * T:(e + 1) * T],
                                             ALU.mult, ALU.mult).then_inc(s_qk, 1)
            dve.wait_ge(bias_in, 32)
            def units(*vs):
                return [lambda v=v: ada_unit(1 + v // 8, v % 8) for v in vs]


            def first_half_gate():
                modulation(1, "ada_b")
                dve.wait_ge(s_mod, 2)
                dve.tensor_scalar(ghalf[:, :], mod[:, 1, 0:8], 0.5, None, ALU.mult).then_inc(s_gate, 1)

            attend(first_heads, {0: units(0), 1: units(1), 2: units(2, 3), 3: units(4), 4: units(5), 5: units(6, 7),
                                 6: [first_half_gate] + units(8), 7: units(9), 8: units(10)})
            for c in range(8):
                u = U["br", c]
                dve.wait_ge(*u.done)
                if c == 0:
                    dve.wait_ge(*taken(U["gp", 7]))
                    dve.wait_ge(*taken(U["gp", 6]))
                if c >= 2:
                    dve.wait_ge(s_merged, 2 * c - 2)
                dve.scalar_tensor_tensor(brt[:, c % 2, 0, :], ga[:, c, :], 1.0, bank(u, 0, T), ALU.add, ALU.mult).then_inc(s_merged, 1)
                dve.scalar_tensor_tensor(brt[:, c % 2, 1, :], gp[:, c, :], 1.0, bank(u, T, 2 * T), ALU.add, ALU.mult)\
                   .then_inc(freed[u.bank], 1)
                dve.wait_ge(s_merged, 2 * c + 1)
                dve.wait_ge(*taken(u))
                dve.tensor_tensor(merged[:, c, :], brt[:, c % 2, 0, :], brt[:, c % 2, 1, :], ALU.add).then_inc(s_merged, 1)
                if c in (1, 3, 5):
                    ada_unit(2, 3 + c // 2)
            dve.wait_ge(s_gate, 1)
            residual_units("wo", ghalf, {c: units(13 + c)[0] for c in (1, 2)})
            modulation(2, "ada_b")
            norm_vector(1)
            norm(1)
            ffn("ffn1", True, 3, "e_ada_b")
            norm(2)
            dve.memset(lf72, 0.0).then_inc(s_cum, 1)
            dve.memset(cum, 1.0).then_inc(s_cum, 1)
            u = U["fglT"]
            dve.wait_ge(*u.done)
            dve.tensor_tensor(lf[:, 0, 0, :], bank(u, 0, 8), col("rows", 0, 8), ALU.add).then_inc(s_forget, 1)
            dve.tensor_tensor(lf[:, 0, 1, :], bank(u, 8, 16), col("rows", 0, 8), ALU.add).then_inc(freed[u.bank], 1)
            dve.wait_ge(s_forget, 4)
            dve.tensor_scalar(lf[:, 2], lf[:, 0], 0.0, None, ALU.min).then_inc(s_forget, 1)
            dve.wait_ge(s_forget, 5)
            dve.wait_ge(s_cum, 2)
            dve.tensor_tensor(lf72[:, :, 0:8], lf[:, 2], lf[:, 1], ALU.subtract).then_inc(s_forget, 1)
            dve.tensor_tensor(lf72[:, :, 64:72], lf[:, 1], lf[:, 2], ALU.subtract).then_inc(s_forget, 1)
            u = U["cum"]
            dve.wait_ge(*u.done)
            dve.tensor_scalar(cum[0:8, :], bank(u, 0, T, 8), 1 / SCALE, None, ALU.mult).then_inc(s_cum, 1)
            dve.wait_ge(sel_in, 16)
            negated = banks[64:72, u.bank:u.bank + 1, 0:T].broadcast_to([8, 8, T])
            dve.scalar_tensor_tensor(sel[64:72, :, :], sel[64:72, :, :], 1 / SCALE, negated, ALU.mult, ALU.mult)\
               .then_inc(freed[u.bank], 1)
            between = {c + 1: [lambda c=c: rope(c, sqT[:, c, :], ("sq", c))] for c in range(4)}
            between[5] = [lambda: rope(4, skT, ("sk", 0))]
            attend(even_heads, between)
            residual_units("eo", mod[:, 4, 0:8])
            norm(3)
            ffn("ffn2", False, 6, "o_ada_b")
            norm(4)
            rope(5, ikT, ("ik", 0))
            for c in range(4):
                rope(6 + c, iqT[:, c, :], ("iq", c))
            for m in range(8):
                dve.wait_ge(s_relu, m + 1)
                if m == 0:
                    dve.wait_ge(*taken(U["iwT"]))
                for j, (lo, hi) in enumerate(((0, HALF), (HALF, TRI))):
                    w = iws[:, j, m:m + 1]
                    if m == 0:
                        dve.tensor_scalar(score[:, lo:hi], relu[:, 0, lo:hi], w, None, ALU.mult).then_inc(s_isum, 1)
                    else:
                        dve.wait_ge(s_isum, 2 * m - 1 + j)
                        dve.scalar_tensor_tensor(score[:, lo:hi], relu[:, m % 2, lo:hi], w, score[:, lo:hi],
                                                 ALU.mult, ALU.add).then_inc(s_isum, 1)
            dve.wait_ge(s_isum, 16)
            dve.tensor_tensor(work, score, causal, ALU.add).then_inc(s_isum, 1)
            dve.wait_ge(s_isum, 17)

            def top_rounds(r0):
                for r in (r0, r0 + 1):
                    for j, (lo, hi) in enumerate(((0, HALF), (HALF, TRI))):
                        if r:
                            dve.wait_ge(s_topk, 4 * r - 1 + j)
                        dve.max(top8[:, j, :], work[:, lo:hi]).then_inc(s_topk, 1)
                    for j, (lo, hi) in enumerate(((0, HALF), (HALF, TRI))):
                        dve.wait_ge(s_topk, 4 * r + 1 + j)
                        dve.match_replace(work[:, lo:hi], top8[:, j, :], work[:, lo:hi], TAKEN).then_inc(s_topk, 1)

            rope(10, dkT[:, 0, :], ("dk", 0))
            top_rounds(0)
            rope(11, dkT[:, 1, :], ("dk", 1))
            top_rounds(2)
            rope(12, dqT[:, 0, :], ("dq", 0))
            top_rounds(4)
            rope(13, dqT[:, 1, :], ("dq", 1))
            top_rounds(6)
            rope(14, dqT[:, 2, :], ("dq", 2))
            dve.wait_ge(s_topk, 32)
            dve.tensor_scalar(dmask, work, TAKEN / 2, -BIG, ALU.is_gt, ALU.mult).then_inc(s_dmask, 1)
            dve.wait_ge(s_dmask, 1)
            dve.tensor_tensor(dmask, dmask, causal, ALU.add).then_inc(s_dmask, 1)
            dve.wait_ge(s_dmask, 2)
            attend(odd_heads, {2 * (c - 3): [lambda c=c: rope(12 + c, dqT[:, c, :], ("dq", c))] for c in range(3, 8)})
            residual_units("oo", mod[:, 7, 0:8])
            norm(5)

            def two(a, n):
                return rt[:, a:a + 2 * n].rearrange("p (a e) -> p a e", a=2)

            picked, lwork, v8, rep8, marked = two(0, 8), two(16, 16), two(48, 8), two(64, 8), two(80, 16)
            lg, den, rden, comb, rank = two(112, 8), rt[:, 128:130], rt[:, 130:132], two(132, 8), two(148, 8)
            count, over, pre, pre2, slotno = rt[:, 164:172], rt[:, 172:188], rt[:, 188:204], rt[:, 204:220], rt[:, 220:236]
            match = rt[:, 236:236 + 16 * EXTRA].rearrange("p (q c) -> p q c", q=EXTRA)
            ranks2, comb2 = two(316, 16), two(348, 16)
            prod = rt[:, 380:380 + 16 * EXTRA].rearrange("p (q c) -> p q c", q=EXTRA)
            chain[0] = 0
            dve.wait_ge(s_o, 20)
            dve.memset(lwork[:, :, 8:16], TAKEN).then_inc(s_route, 1)
            dve.memset(rep8[:, :, 2:8], TAKEN).then_inc(s_route, 1)
            u = U["routerT"]
            dve.wait_ge(*u.done)
            dve.tensor_tensor(lwork[:, 0, 0:8], bank(u, 0, 8), col("rows", 16, 24), ALU.add).then_inc(s_route, 1)
            dve.tensor_tensor(lwork[:, 1, 0:8], bank(u, 8, 16), col("rows", 16, 24), ALU.add).then_inc(freed[u.bank], 1)
            dve.wait_ge(s_route, 3)
            dve.wait_ge(*taken(u))
            dve.max(v8[:, 0, :], lwork[:, 0, 0:8]).then_inc(s_route, 1)
            dve.max(v8[:, 1, :], lwork[:, 1, 0:8]).then_inc(s_route, 1)
            chain[0] = 5
            dve.wait_ge(s_route, 5)
            link(dve.tensor_copy(rep8[:, :, 0:2], v8[:, :, 0:2]), s_route)
            for tile in range(2):
                link(dve.match_replace(marked[:, tile, :], rep8[:, tile, :], lwork[:, tile, :], -TAKEN), s_route)
            link(dve.tensor_scalar(picked, marked[:, :, 0:8], -TAKEN / 2, None, ALU.is_gt), s_route)
            assert chain[0] == 9
            for tile in range(2):
                link(dve.tensor_scalar(lg[:, tile, :], lwork[:, tile, 0:8], v8[:, tile, 0:1], None, ALU.subtract), s_route)
            u = U["ranks"]
            dve.wait_ge(*u.done)
            link(dve.tensor_tensor(rank, bank(u, 0, 16).rearrange("p (a e) -> p a e", a=2), picked, ALU.mult), s_route)
            iota = mat("iota")
            for tile in range(2):
                dve.tensor_scalar(pick[:, tile, :], iota, rank[:, tile, 0:1], None, ALU.is_equal).then_inc(s_pick, 1)
            dve.tensor_copy(count, bank(u, 16, 24)).then_inc(freed[u.bank], 1)
            dve.wait_ge(*taken(u))
            link(dve.tensor_scalar(over[:, 0:8], count, float(CAP), None, ALU.is_gt), s_route)
            link(dve.tensor_scalar(over[:, 8:16], count, float(2 * CAP), None, ALU.is_gt), s_route)
            link(dve.tensor_reduce(rt[:, 480:481], over, AX, ALU.add), s_route)
            dve.tensor_scalar(ints[:, NTAB:NTAB + 1], rt[:, 480:481], float(EXPERTS), None, ALU.add).then_inc(s_passes, 1)
            dve.wait_ge(s_gexp, 1)
            link(dve.tensor_tensor(comb, lg, picked, ALU.mult), s_route)
            link(dve.tensor_reduce(den, comb, AX, ALU.add), s_route)
            link(dve.reciprocal(rden, den), s_route)
            for tile in range(2):
                link(dve.tensor_scalar(comb[:, tile, :], comb[:, tile, :], rden[:, tile:tile + 1], None, ALU.mult), s_route)
            link(dve.memset(tab, 0.0), s_route)
            for tile in range(2):
                link(dve.tensor_copy(tab[:, 0:EXPERTS, tile], rank[:, tile, :]), s_route)
                link(dve.tensor_copy(tab[:, 0:EXPERTS, 2 + tile], comb[:, tile, :]), s_route)
            link(dve.tensor_copy(cur, tab[:, 0, :]), s_route)
            m0 = U["moe"]
            before = [len(range(s, m0.pos, RING)) if s < RING else 0 for s in range(MSLOTS)]
            def extra_passes():
                link(dve.tensor_copy(pre, over), s_route)
                a, b = pre, pre2
                for shift in (1, 2, 4, 8):
                    link(dve.tensor_copy(b[:, 0:shift], a[:, 0:shift]), s_route)
                    link(dve.tensor_tensor(b[:, shift:16], a[:, shift:16], a[:, 0:16 - shift], ALU.add), s_route)
                    a, b = b, a
                link(dve.tensor_tensor(slotno, a, over, ALU.mult), s_route)
                for q in range(EXTRA):
                    link(dve.tensor_scalar(match[:, q, :], slotno, float(q + 1), None, ALU.is_equal), s_route)
                cand_expert, cand_block = mat("small", 0, 16), mat("small", 16, 32)
                for tile in range(2):
                    for half in range(2):
                        link(dve.scalar_tensor_tensor(ranks2[:, tile, 8 * half:8 * half + 8], cand_block[:, 8 * half:8 * half + 8],
                                                      -float(CAP), rank[:, tile, :], ALU.mult, ALU.add), s_route)
                        link(dve.tensor_copy(comb2[:, tile, 8 * half:8 * half + 8], comb[:, tile, :]), s_route)
                extra = slice(EXPERTS, EXPERTS + EXTRA)
                for k, source in enumerate((ranks2[:, 0, :], ranks2[:, 1, :], comb2[:, 0, :], comb2[:, 1, :], cand_expert)):
                    wide = source.rearrange("p (o c) -> p o c", o=1).broadcast_to([P, EXTRA, 16])
                    link(dve.tensor_tensor(prod, match, wide, ALU.mult), s_route)
                    if k < 4:
                        link(dve.tensor_reduce(tab[:, extra, k], prod, AX, ALU.add), s_route)
                link(dve.tensor_reduce(rt[:, 460:460 + EXTRA], prod, AX, ALU.add), s_route)
                link(dve.tensor_copy(ints[:, 0:EXPERTS], cand_expert[:, 0:EXPERTS]), s_route)
                link(dve.tensor_copy(ints[:, extra], rt[:, 460:460 + EXTRA]), s_route)
                dve.engine_nop().then_inc(s_routed, 1)

            def expert_pass(p, first=False):
                for tile in range(2):
                    dve.tensor_scalar(cpick[:, tile, :], iota, cur[:, tile:tile + 1], cur[:, 2 + tile:3 + tile],
                                      ALU.is_equal, ALU.mult).then_inc(s_cpick, 1)
                for f in range(EF):
                    b = use_of(f) % 2
                    dve.wait_ge(s_silu, 2 * FC + EF * p + f + 1)
                    dve.wait_ge(slot_used[3 * f + 1], before[3 * f + 1] + p + 1)
                    dve.tensor_tensor(ehid[:, f % 2, :], esg[:, f % 2, :], banks[:, b, T:T + CAP], ALU.mult).then_inc(freed[b], 1)
                    if f == 1:
                        dve.wait_ge(aux_done, m0.done + 3 * p + 1)
                        dve.tensor_copy(pickT, banks[0:CAP, 0, 0:T]).then_inc(freed[0], 1)
                        if first:
                            extra_passes()
                    if f == 3:
                        dve.wait_ge(s_cpick, 2 * p + 2)
                        dve.tensor_copy(cur, tab[:, bass.ds(p + 1, 1), :].rearrange("p a n -> p (a n)")).then_inc(s_cur, 1)
                        dve.wait_ge(s_cur, p + 1)
                        for tile in range(2):
                            dve.tensor_scalar(pick[:, tile, :], iota, cur[:, tile:tile + 1], None, ALU.is_equal).then_inc(s_pick, 1)
                dve.wait_ge(aux_done, m0.done + 3 * p + 2)
                dve.tensor_copy(hg[:, 0:4, :].rearrange("p a n -> p (a n)"), banks[:, 0, 0:4 * CAP]).then_inc(freed[0], 1)
                dve.wait_ge(slot_used[MSLOTS - 1], before[MSLOTS - 1] + p + 1)
                dve.tensor_copy(y_tok[:, 512:1024], banks[0:CAP, 3, :]).then_inc(s_y_dve, 1)

            expert_pass(0, True)
            passes = dve.value_load(ints[0:1, NTAB:NTAB + 1], min_val=EXPERTS, max_val=EXPERTS + EXTRA)
            with dve.Fori(1, passes) as p:
                expert_pass(p)
            residual_acc(2)
            norm(6)


def _bucket(dist):
    n = np.maximum(dist, 0)
    nf = np.maximum(n, 1).astype(np.float32)
    large = 16 + (np.log(nf / np.float32(16)) / np.float32(np.log(8.0)) * np.float32(16)).astype(np.int32)
    return np.where(n < 16, n, np.minimum(large, 31))


def _constants():
    mats = np.zeros((P, NMATS), np.float32)

    def put(name, value):
        at, n = MATS[name]
        mats[:value.shape[0], at:at + n] = value

    p, t = np.arange(P)[:, None], np.arange(T)[None, :]
    put("ident", np.eye(P))
    put("heads", (p // HD == np.arange(P)[None, :] // HD) * 1.0)
    k, m = p, np.arange(P)[None, :]
    put("rotate", (k == m - 32) * (m % HD >= 32) * 1.0 - (k == m + 32) * (m % HD < 32) * 1.0)
    dist = np.concatenate([p - np.arange(HALF)[None, :], HALF + p - t], 1)
    put("causal", np.where(dist >= 0, 0.0, -BIG))
    put("band", np.where((dist >= 0) & (dist < 128), 0.0, -BIG))
    put("upto", (p <= t) * 1.0)
    put("iota", np.broadcast_to(np.arange(1, CAP + 1), (P, CAP)))
    small = np.zeros((P, 64))
    small[:, 0:16] = np.arange(16) % 8
    small[:, 16:32] = 1 + np.arange(16) // 8
    put("small", small)
    onehot = np.zeros((33, 512), np.float32)
    d = 255 - np.arange(512)
    onehot[_bucket(d), np.arange(512)] = d >= 0
    onehot[32] = np.where(d >= 0, 0.0, -BIG)
    pool = np.zeros((T, 4, T), np.float32)
    src, dst = np.arange(T)[:, None], np.arange(T)[None, :]
    for g, w in enumerate((2, 4, 8, 16)):
        inside = (src <= dst) & (src > dst - w)
        pool[:, g, :] = inside / np.minimum(dst + 1, w).astype(np.float32) - (src == dst)
    pool = np.ascontiguousarray(pool.reshape(2, P, 4, T).transpose(1, 0, 2, 3))
    sel = np.zeros((72, 8, T), np.float32)
    sel[np.arange(8), np.arange(8)] = 1.0
    sel[64 + np.arange(8), np.arange(8)] = 1.0
    inv_freq = (np.float32(10000.0) ** (-np.arange(32, dtype=np.float32) / np.float32(32))).astype(np.float32)
    return mats, onehot, pool, sel, inv_freq


def _tiles(w, columns=None):
    w = w if columns is None else w[:, columns]
    return w.reshape(KC, P, -1, P).transpose(2, 1, 0, 3).reshape(-1, P, SLOT)


def _rows(w, slots, width):
    return w.reshape(slots, KC // slots, P, width).transpose(0, 2, 1, 3).reshape(slots, P, SLOT)


def _ffn(gate, up, down):
    return np.stack([_tiles(gate), _tiles(up), down.reshape(-1, P, SLOT)], 1).reshape(-1, P, SLOT)


def _columns(v):
    return v.reshape(-1, P).T


def kernel(**inputs):
    import concourse.bacc as bacc
    from concourse.bass_utils import run_bass_kernel_spmd

    a = {name: np.asarray(value) for name, value in inputs.items()}
    f = lambda name: a[name][0]
    mats, onehot, pool, sel, inv_freq = _constants()
    swa = np.concatenate([np.arange(64) + 64 * (j + 4 * half) for j in range(4) for half in range(2)])
    dsa = np.concatenate([np.arange(64) + 64 * (8 * (j // 4) + j % 4 + 4 * half) for j in range(8) for half in range(2)])
    w_in, ew, ow = f("w_in"), f("e_w_in_2"), f("o_w_in_2")
    branch = np.concatenate([f("w_branch_attn").reshape(4, P, 8, P), f("w_branch_pool").reshape(4, P, 8, P)], 0)
    ada = np.concatenate([f(n).T.reshape(-1, 2, P, D).transpose(0, 2, 1, 3) for n in ("ada_w", "e_ada_w_2", "o_ada_w_2")])
    half = 2816
    parts = [
        ada[0:8].transpose(0, 2, 1, 3).reshape(16, P, SLOT),
        _tiles(w_in[:, 0:1024]), _rows(w_in[:, 1024:1536], 4, 512), _rows(w_in[:, 1536:2048], 4, 512),
        _tiles(w_in[:, 2048:4096]), branch.transpose(2, 1, 0, 3).reshape(8, P, SLOT), _tiles(f("w_out")),
        _ffn(f("w_up")[:, :half], f("w_up")[:, half:], f("w_down")),
        _tiles(ew[:, 0:1024]), _rows(ew[:, 1024:1536], 4, 512), _tiles(ew[:, 1544:2056], swa), _tiles(ew[:, 2056:2184]),
        _rows(ew[:, 2184:2312], 1, 128), _tiles(f("e_w_out_2")[np.concatenate([np.arange(512), 512 + swa])]),
        _ffn(f("e_ffn_gate_2"), f("e_ffn_up_2"), f("e_ffn_down_2")),
        _tiles(np.concatenate([ow[:, 2048:2112]] * 2, 1)), _tiles(ow[:, 1536:2048]), _tiles(ow[:, 1024:1280]),
        _rows(ow[:, 1280:1536], 2, 256), _tiles(ow[:, 0:1024], dsa), _tiles(f("o_w_out_2")[dsa]),
    ]
    stream = np.concatenate(parts)
    experts = np.concatenate([_ffn(f("o_exp_gate_2")[e], f("o_exp_up_2")[e], f("o_exp_down_2")[e]) for e in range(EXPERTS)])
    conv = np.stack([*f("conv_w"), f("conv_b")]).reshape(4, 2, FC, P).transpose(3, 2, 1, 0).reshape(P, 8 * FC)
    wide = lambda v: np.broadcast_to(v, (P, v.size))
    small = lambda w: w.reshape(KC, P, 8).transpose(1, 0, 2).reshape(P, 64)
    cols = np.concatenate([
        *[_columns(a[n]) for n in ("norm1_g", "norm2_g", "e_norm_mix_2", "e_norm_ffn_2", "o_norm_mix_2", "o_norm_ffn_2",
                                   "final_norm_2", "ada_b", "e_ada_b_2", "o_ada_b_2", "pool_scale")],
        np.tile(f("q_norm_g"), 2)[:, None], np.tile(f("k_norm_g"), 2)[:, None], conv, 
        np.tile(inv_freq, 4)[:, None], wide(f("e_forget_b_2")), wide(f("e_sinks_2")), wide(f("o_router_b_2")),
        small(ew[:, 1536:1544]), small(ow[:, 2112:2120]), small(f("o_router_w_2"))], 1)
    relb = np.concatenate([a["rel_bias"], np.ones((1, 8), np.float32)])
    arrays = {
        "xT": a["x"][0].T.reshape(KC, P, T).transpose(1, 0, 2), "cols": cols, "mats": mats,
        "positions": np.broadcast_to(a["positions_2"].reshape(1, T), (P, T)), "onehot": onehot,
        "relb": np.broadcast_to(relb[:, :, None], (33, 8, P)), "sel": sel, "poolA": pool,
        "poolw": f("pool_w").transpose(1, 0, 2), "stream": stream, "cond": np.concatenate([a["c"], a["c_2"]]), "ada": ada[8:], "experts": experts}
    arrays = {name: np.ascontiguousarray(v) for name, v in arrays.items()}
    nc = bacc.Bacc("TRN2", target_bir_lowering=False, num_devices=1)
    args = [nc.dram_tensor(name, v.shape, mybir.dt.from_np(v.dtype), kind="ExternalInput").ap() for name, v in arrays.items()]
    out = nc.dram_tensor("out_0_dram", (P, KC, T), F32, kind="ExternalOutput").ap()
    program(nc, *args, out)
    r = run_bass_kernel_spmd(nc, [arrays], core_ids=[0])
    y = r.results[0]["out_0_dram"]
    return np.ascontiguousarray(y.transpose(2, 1, 0).reshape(1, T, D))
```
